# Optimizing a Trainium2 kernel written in Bass

```python
import jax, jax.numpy as jnp
from jax import lax
import numpy as np
import math

D_MODEL = 1024
BATCH = 1
SEQ = 256
DEPTH = 1

CHUNK = 64
EXPAND = 2
E_A = EXPAND * D_MODEL // 2
E_B = EXPAND * D_MODEL // 2
A_GROUPS = 8
A_BLOCK = 128
B_GROUPS = 8
CONV_WIDTH = 31
PLE_DIM = 256
NORM_EPS = 1e-6
LN_EPS = 1e-5
N_IN = 3 * E_A + 3 * E_B + 2 * D_MODEL
SPLIT_IDX = [E_A, 2 * E_A, 3 * E_A, 3 * E_A + E_B, 3 * E_A + 2 * E_B,
             3 * E_A + 3 * E_B, 3 * E_A + 3 * E_B + D_MODEL]


def _rmsnorm(x, g):
    xf = x.astype(jnp.float32)
    y = xf * lax.rsqrt(jnp.mean(xf * xf, axis=-1, keepdims=True) + NORM_EPS)
    return (y * g.astype(jnp.float32)).astype(x.dtype)

def _normalize(x):
    xf = x.astype(jnp.float32)
    mu = jnp.mean(xf, axis=-1, keepdims=True)
    var = jnp.mean(jnp.square(xf - mu), axis=-1, keepdims=True)
    return (xf - mu) * lax.rsqrt(var + LN_EPS)

def _chunk_causal_mask():
    c = jnp.arange(A_BLOCK) // CHUNK
    return c[:, None] >= c[None, :]

def _spatial_gating_branch(u, v, z, ln_g, ln_b, ws, bs):
    b_, s_, _ = v.shape
    v = (_normalize(v) * ln_g.astype(jnp.float32) + ln_b.astype(jnp.float32)).astype(u.dtype)
    ws = jnp.where(_chunk_causal_mask()[None], ws, jnp.zeros_like(ws))
    vb = v.reshape(b_, s_ // A_BLOCK, A_BLOCK, A_GROUPS, E_A // A_GROUPS)
    mixed = jnp.einsum('gij,bnjgc->bnigc', ws, vb) + bs.T[:, :, None]
    mixed = mixed.reshape(b_, s_, E_A)
    return u * mixed * jax.nn.silu(z)

def _conformer_conv_branch(a, a_gate, z, conv_w, conv_b, gn_g, gn_b):
    h = a * jax.nn.sigmoid(a_gate)
    h = lax.conv_general_dilated(
        h, conv_w[:, None, :].astype(h.dtype), window_strides=(1,),
        padding=[(CONV_WIDTH - 1, 0)], dimension_numbers=('NWC', 'WIO', 'NWC'),
        feature_group_count=E_B) + conv_b
    b_, s_, _ = h.shape
    hn = _normalize(h.reshape(b_, s_, B_GROUPS, E_B // B_GROUPS)).reshape(b_, s_, E_B)
    hn = (hn * gn_g.astype(jnp.float32) + gn_b.astype(jnp.float32)).astype(a.dtype)
    return jax.nn.silu(hn) * jax.nn.silu(z)

def first_inputs(seed: int = 0) -> dict:
    key = jax.random.key(seed)
    ks = jax.random.split(key, 20)
    f32 = jnp.float32
    nrm = lambda k, shape, scale: jax.random.normal(k, shape, f32) * scale
    return {
        "x": nrm(ks[0], (BATCH, SEQ, D_MODEL), 1.0),
        "p": nrm(ks[1], (DEPTH, BATCH, SEQ, PLE_DIM), 1.0),
        "norm_g": 1.0 + nrm(ks[2], (DEPTH, D_MODEL), 0.05),
        "w_in": nrm(ks[3], (DEPTH, D_MODEL, N_IN), D_MODEL ** -0.5),
        "b_in": nrm(ks[4], (DEPTH, N_IN), 0.02),
        "a_ln_g": 1.0 + nrm(ks[5], (DEPTH, E_A), 0.05),
        "a_ln_b": nrm(ks[6], (DEPTH, E_A), 0.02),
        "a_ws": nrm(ks[7], (DEPTH, A_GROUPS, A_BLOCK, A_BLOCK), A_BLOCK ** -0.5),
        "a_bs": 1.0 + nrm(ks[8], (DEPTH, A_GROUPS, A_BLOCK), 0.1),
        "b_conv_w": nrm(ks[9], (DEPTH, CONV_WIDTH, E_B), CONV_WIDTH ** -0.5),
        "b_conv_b": nrm(ks[10], (DEPTH, E_B), 0.02),
        "b_gn_g": 1.0 + nrm(ks[11], (DEPTH, E_B), 0.05),
        "b_gn_b": nrm(ks[12], (DEPTH, E_B), 0.02),
        "w_pa": nrm(ks[13], (DEPTH, E_A, D_MODEL), E_A ** -0.5),
        "w_pb": nrm(ks[14], (DEPTH, E_B, D_MODEL), E_B ** -0.5),
        "w_out": nrm(ks[15], (DEPTH, D_MODEL, D_MODEL), D_MODEL ** -0.5),
        "ple_norm_g": 1.0 + nrm(ks[16], (DEPTH, D_MODEL), 0.05),
        "w_ple_gate": nrm(ks[17], (DEPTH, D_MODEL, D_MODEL), D_MODEL ** -0.5),
        "w_ple": nrm(ks[18], (DEPTH, PLE_DIM, D_MODEL), PLE_DIM ** -0.5),
        "final_g": 1.0 + nrm(ks[19], (D_MODEL,), 0.05),
    }

def first_block(x, p, norm_g, w_in, b_in, a_ln_g, a_ln_b, a_ws, a_bs, b_conv_w, b_conv_b,
              b_gn_g, b_gn_b, w_pa, w_pb, w_out, ple_norm_g, w_ple_gate, w_ple, final_g):
    for i in range(DEPTH):
        h = _rmsnorm(x, norm_g[i])
        proj = jnp.einsum('bsd,dn->bsn', h, w_in[i]) + b_in[i]
        u, v, za, ab, ab_gate, zb, g_a, g_b = jnp.split(proj, SPLIT_IDX, axis=-1)
        y_a = _spatial_gating_branch(jax.nn.gelu(u), jax.nn.gelu(v), za,
                                     a_ln_g[i], a_ln_b[i], a_ws[i], a_bs[i])
        y_b = _conformer_conv_branch(ab, ab_gate, zb, b_conv_w[i], b_conv_b[i],
                                     b_gn_g[i], b_gn_b[i])
        merged = (jax.nn.sigmoid(g_a) * jnp.einsum('bse,ed->bsd', y_a, w_pa[i])
                  + jax.nn.sigmoid(g_b) * jnp.einsum('bse,ed->bsd', y_b, w_pb[i]))
        x = x + jnp.einsum('bsd,de->bse', merged, w_out[i])
        ple_gate = jax.nn.sigmoid(jnp.einsum('bsd,de->bse', _rmsnorm(x, ple_norm_g[i]), w_ple_gate[i]))
        x = x + ple_gate * jnp.einsum('bsk,kd->bsd', p[i], w_ple[i])
    return _rmsnorm(x, final_g)


HEAD_DIM = 64
N_HEADS_A = 8
N_HEADS_B = 8
D_A = N_HEADS_A * HEAD_DIM
D_B = N_HEADS_B * HEAD_DIM
N_IDX_HEADS = 8
IDX_DIM = 64
D_RNN = 512
N_RNN_BLOCKS = 8
RNN_BLOCK = D_RNN // N_RNN_BLOCKS
CONV_WIDTH_2 = 4
LRU_C = 8.0
D_FF = 4 * D_MODEL
MOBA_BLOCK = 256
MOBA_TOPK = 3
DSA_MAX_TOPK = 256
Q_BLOCK = 128
N_BUCKETS = 32
MAX_DISTANCE = 128
N_BRANCHES = 3
N_ATTN_HEADS = N_HEADS_A + N_HEADS_B
EPS = 1e-6
NEG = -1e30

IN_SPLITS = (D_A, D_A, D_A,
             D_B, D_B, D_B,
             N_IDX_HEADS * IDX_DIM,
             IDX_DIM,
             N_IDX_HEADS,
             D_RNN, D_RNN,
             N_BRANCHES * D_MODEL)
D_IN = sum(IN_SPLITS)
IN_OFFSETS = tuple(int(o) for o in np.cumsum(IN_SPLITS)[:-1])


def rms_norm(x, g):
    xf = x.astype(jnp.float32)
    y = xf * lax.rsqrt(jnp.mean(xf * xf, axis=-1, keepdims=True) + EPS)
    return (y * g.astype(jnp.float32)).astype(x.dtype)

def t5_bucket(dist):
    n = jnp.maximum(dist, 0)
    max_exact = N_BUCKETS // 2
    nf = jnp.maximum(n, 1).astype(jnp.float32)
    large = max_exact + (jnp.log(nf / max_exact) / math.log(MAX_DISTANCE / max_exact)
                         * (N_BUCKETS - max_exact)).astype(jnp.int32)
    large = jnp.minimum(large, N_BUCKETS - 1)
    return jnp.where(n < max_exact, n, large)

def moba_attention(q, k, v, bias_tab):
    B, S, H, dh = q.shape
    nb = -(-S // MOBA_BLOCK)
    pad = nb * MOBA_BLOCK - S
    kp = jnp.pad(k, ((0, 0), (0, pad), (0, 0), (0, 0)))
    vp = jnp.pad(v, ((0, 0), (0, pad), (0, 0), (0, 0)))
    kblk = kp.reshape(B, nb, MOBA_BLOCK, H, dh).transpose(0, 3, 1, 2, 4)
    vblk = vp.reshape(B, nb, MOBA_BLOCK, H, dh).transpose(0, 3, 1, 2, 4)
    kmean = jnp.mean(kblk, axis=3)
    n_sel = min(MOBA_TOPK, nb)
    scale = dh ** -0.5
    b_ix = jnp.arange(B)[:, None, None, None]
    h_ix = jnp.arange(H)[None, None, :, None]
    blk_ids = jnp.arange(nb)
    bias_t = bias_tab.T

    def one_block(qb):
        t0 = qb * Q_BLOCK
        cur = t0 // MOBA_BLOCK
        t = t0 + jnp.arange(Q_BLOCK)
        qq = lax.dynamic_slice_in_dim(q, t0, Q_BLOCK, axis=1)
        gate = jnp.einsum('bqhd,bhnd->bqhn', qq, kmean).astype(jnp.float32)
        gate = jnp.where(blk_ids < cur, gate, NEG)
        _, sel = lax.top_k(gate, n_sel)
        sel_ok = sel < cur
        kg = kblk[b_ix, h_ix, sel]
        vg = vblk[b_ix, h_ix, sel]
        s_past = jnp.einsum('bqhd,bqhnkd->bqhnk', qq, kg).astype(jnp.float32) * scale
        pos_past = sel[..., None] * MOBA_BLOCK + jnp.arange(MOBA_BLOCK)
        bias_past = bias_t[h_ix[..., None], t5_bucket(t[None, :, None, None, None] - pos_past)]
        s_past = jnp.where(sel_ok[..., None], s_past + bias_past, NEG)
        k_own = lax.dynamic_slice_in_dim(kp, cur * MOBA_BLOCK, MOBA_BLOCK, axis=1)
        v_own = lax.dynamic_slice_in_dim(vp, cur * MOBA_BLOCK, MOBA_BLOCK, axis=1)
        rel = t[:, None] - (cur * MOBA_BLOCK + jnp.arange(MOBA_BLOCK))[None, :]
        bias_own = bias_tab[t5_bucket(rel)].transpose(0, 2, 1)[None]
        s_own = jnp.einsum('bqhd,bkhd->bqhk', qq, k_own).astype(jnp.float32) * scale + bias_own
        s_own = jnp.where((rel >= 0)[None, :, None, :], s_own, NEG)
        logits = jnp.concatenate([s_past.reshape(B, Q_BLOCK, H, n_sel * MOBA_BLOCK), s_own], axis=-1)
        p = jax.nn.softmax(logits, axis=-1).astype(v.dtype)
        p_past = p[..., :n_sel * MOBA_BLOCK].reshape(B, Q_BLOCK, H, n_sel, MOBA_BLOCK)
        p_own = p[..., n_sel * MOBA_BLOCK:]
        return (jnp.einsum('bqhnk,bqhnkd->bqhd', p_past, vg)
                + jnp.einsum('bqhk,bkhd->bqhd', p_own, v_own))

    out = lax.map(one_block, jnp.arange(S // Q_BLOCK))
    return out.transpose(1, 0, 2, 3, 4).reshape(B, S, H * dh)

def dsa_attention(q, k, v, qi, ki, wi, bias_tab):
    B, S, H, dh = q.shape
    n_keep = min(DSA_MAX_TOPK, S // 4)
    scale = dh ** -0.5
    idx_scale = (N_IDX_HEADS ** -0.5) * (IDX_DIM ** -0.5)
    s_all = jnp.arange(S)

    def one_block(qb):
        t0 = qb * Q_BLOCK
        t = t0 + jnp.arange(Q_BLOCK)
        qq = lax.dynamic_slice_in_dim(q, t0, Q_BLOCK, axis=1)
        qiq = lax.dynamic_slice_in_dim(qi, t0, Q_BLOCK, axis=1)
        wq = lax.dynamic_slice_in_dim(wi, t0, Q_BLOCK, axis=1)
        dots = jnp.einsum('bqhd,bsd->bqhs', qiq, ki)
        score = jnp.einsum('bqh,bqhs->bqs', wq, jax.nn.relu(dots)).astype(jnp.float32) * idx_scale
        score = jnp.where((s_all[None, :] <= t[:, None])[None], score, NEG)
        _, idx = lax.top_k(score, n_keep)
        ok = idx <= t[None, :, None]
        kg = jax.vmap(lambda kk, ii: kk[ii])(k, idx)
        vg = jax.vmap(lambda vv, ii: vv[ii])(v, idx)
        bias = bias_tab[t5_bucket(t[None, :, None] - idx)].transpose(0, 1, 3, 2)
        logits = jnp.einsum('bqhd,bqkhd->bqhk', qq, kg).astype(jnp.float32) * scale + bias
        logits = jnp.where(ok[:, :, None, :], logits, NEG)
        p = jax.nn.softmax(logits, axis=-1).astype(v.dtype)
        return jnp.einsum('bqhk,bqkhd->bqhd', p, vg)

    out = lax.map(one_block, jnp.arange(S // Q_BLOCK))
    return out.transpose(1, 0, 2, 3, 4).reshape(B, S, H * dh)

def causal_depthwise_conv(x, w, b):
    S = x.shape[1]
    xp = jnp.pad(x, ((0, 0), (CONV_WIDTH_2 - 1, 0), (0, 0)))
    y = b
    for i in range(CONV_WIDTH_2):
        y = y + w[i] * xp[:, i:i + S]
    return y

def rg_lru(x, w_r, b_r, w_i, b_i, lam):
    B, S, C = x.shape
    xb = x.reshape(B, S, N_RNN_BLOCKS, RNN_BLOCK)
    r = jax.nn.sigmoid(jnp.einsum('bsnc,ncd->bsnd', xb, w_r).reshape(B, S, C) + b_r)
    i = jax.nn.sigmoid(jnp.einsum('bsnc,ncd->bsnd', xb, w_i).reshape(B, S, C) + b_i)
    log_a = -LRU_C * r.astype(jnp.float32) * jax.nn.softplus(-lam.astype(jnp.float32))
    a = jnp.exp(log_a)
    u = jnp.sqrt(-jnp.expm1(2.0 * log_a)) * (i * x).astype(jnp.float32)

    def combine(left, right):
        a1, b1 = left
        a2, b2 = right
        return a1 * a2, a2 * b1 + b2

    _, h = lax.associative_scan(combine, (a, u), axis=1)
    return h.astype(x.dtype)

def token_mixer(xn, w_in, conv_w, conv_b, w_r, b_r, w_i, b_i, lam, w_pa, w_pb, w_pc, w_o, rel_bias):
    B, S, _ = xn.shape
    proj = xn @ w_in
    (qa, ka, va, qb, kb, vb, qi, ki, wi, xc, yc, gates) = jnp.split(proj, IN_OFFSETS, axis=-1)
    heads_a = lambda z: z.reshape(B, S, N_HEADS_A, HEAD_DIM)
    heads_b = lambda z: z.reshape(B, S, N_HEADS_B, HEAD_DIM)
    y_a = moba_attention(heads_a(qa), heads_a(ka), heads_a(va), rel_bias[:, :N_HEADS_A])
    y_b = dsa_attention(heads_b(qb), heads_b(kb), heads_b(vb),
                        qi.reshape(B, S, N_IDX_HEADS, IDX_DIM), ki, wi, rel_bias[:, N_HEADS_A:])
    y_c = rg_lru(causal_depthwise_conv(xc, conv_w, conv_b), w_r, b_r, w_i, b_i, lam) * jax.nn.gelu(yc)
    g = jax.nn.sigmoid(gates).reshape(B, S, N_BRANCHES, D_MODEL)
    merged = g[:, :, 0] * (y_a @ w_pa) + g[:, :, 1] * (y_b @ w_pb) + g[:, :, 2] * (y_c @ w_pc)
    return merged @ w_o

def squared_relu_mlp(xn, w_up, w_down):
    return jnp.square(jax.nn.relu(xn @ w_up)) @ w_down

def second_inputs(seed: int = 0) -> dict:
    key = jax.random.key(seed)
    ks = jax.random.split(key, 20)
    f32 = jnp.float32
    nrm = lambda k, shape, s: jax.random.normal(k, shape, f32) * s
    u = jax.random.uniform(ks[10], (DEPTH, D_RNN), f32, minval=0.9, maxval=0.999)
    a = u ** (1.0 / LRU_C)
    lam = jnp.log(a) - jnp.log1p(-a)
    return {
        "x": nrm(ks[0], (BATCH, SEQ, D_MODEL), 1.0),
        "rel_bias": nrm(ks[1], (N_BUCKETS, N_ATTN_HEADS), 0.5),
        "norm_mix_g": 1.0 + nrm(ks[2], (DEPTH, D_MODEL), 0.05),
        "w_in": nrm(ks[3], (DEPTH, D_MODEL, D_IN), D_MODEL ** -0.5),
        "conv_w": nrm(ks[4], (DEPTH, CONV_WIDTH_2, D_RNN), CONV_WIDTH_2 ** -0.5),
        "conv_b": nrm(ks[5], (DEPTH, D_RNN), 0.02),
        "w_r": nrm(ks[6], (DEPTH, N_RNN_BLOCKS, RNN_BLOCK, RNN_BLOCK), RNN_BLOCK ** -0.5),
        "b_r": nrm(ks[7], (DEPTH, D_RNN), 0.1),
        "w_i": nrm(ks[8], (DEPTH, N_RNN_BLOCKS, RNN_BLOCK, RNN_BLOCK), RNN_BLOCK ** -0.5),
        "b_i": nrm(ks[9], (DEPTH, D_RNN), 0.1),
        "lru_lambda": lam,
        "w_pa": nrm(ks[11], (DEPTH, D_A, D_MODEL), D_A ** -0.5),
        "w_pb": nrm(ks[12], (DEPTH, D_B, D_MODEL), D_B ** -0.5),
        "w_pc": nrm(ks[13], (DEPTH, D_RNN, D_MODEL), D_RNN ** -0.5),
        "w_o": nrm(ks[14], (DEPTH, D_MODEL, D_MODEL), D_MODEL ** -0.5),
        "norm_mlp_g": 1.0 + nrm(ks[15], (DEPTH, D_MODEL), 0.05),
        "w_up": nrm(ks[16], (DEPTH, D_MODEL, D_FF), D_MODEL ** -0.5),
        "w_down": nrm(ks[17], (DEPTH, D_FF, D_MODEL), D_FF ** -0.5),
        "final_norm_g": 1.0 + nrm(ks[18], (D_MODEL,), 0.05),
    }

def second_block(x, rel_bias, norm_mix_g, w_in, conv_w, conv_b, w_r, b_r, w_i, b_i, lru_lambda,
              w_pa, w_pb, w_pc, w_o, norm_mlp_g, w_up, w_down, final_norm_g):
    for l in range(DEPTH):
        x = x + token_mixer(rms_norm(x, norm_mix_g[l]), w_in[l], conv_w[l], conv_b[l],
                            w_r[l], b_r[l], w_i[l], b_i[l], lru_lambda[l],
                            w_pa[l], w_pb[l], w_pc[l], w_o[l], rel_bias)
        x = x + squared_relu_mlp(rms_norm(x, norm_mlp_g[l]), w_up[l], w_down[l])
    return rms_norm(x, final_norm_g)


def setup_inputs(seed=0):
    out = dict(first_inputs(seed))
    for name, value in second_inputs(seed + 1).items():
        if name != "x":
            out[name + "_2"] = value
    return out


def reference(
    x, p, norm_g, w_in, b_in, a_ln_g, a_ln_b, a_ws, a_bs, b_conv_w, b_conv_b, b_gn_g, b_gn_b,
    w_pa, w_pb, w_out, ple_norm_g, w_ple_gate, w_ple, final_g, rel_bias_2, norm_mix_g_2, w_in_2,
    conv_w_2, conv_b_2, w_r_2, b_r_2, w_i_2, b_i_2, lru_lambda_2, w_pa_2, w_pb_2, w_pc_2, w_o_2,
    norm_mlp_g_2, w_up_2, w_down_2, final_norm_g_2,
):
    x = first_block(
        x, p, norm_g, w_in, b_in, a_ln_g, a_ln_b, a_ws, a_bs, b_conv_w, b_conv_b, b_gn_g,
        b_gn_b, w_pa, w_pb, w_out, ple_norm_g, w_ple_gate, w_ple, final_g,
    )
    return second_block(
        x, rel_bias_2, norm_mix_g_2, w_in_2, conv_w_2, conv_b_2, w_r_2, b_r_2, w_i_2, b_i_2,
        lru_lambda_2, w_pa_2, w_pb_2, w_pc_2, w_o_2, norm_mlp_g_2, w_up_2, w_down_2,
        final_norm_g_2,
    )


_drawn_inputs = setup_inputs


def setup_inputs(seed=0):
    import zlib

    import numpy as np

    out = dict(_drawn_inputs(seed))
    spreads = {}
    factors = {'b_in': 3.315,
     'a_ln_g': 3.936,
     'a_ln_b': 6.404,
     'b_conv_b': 4.24,
     'b_gn_g': 3.392,
     'b_gn_b': 6.577,
     'ple_norm_g': 9.977,
     'b_r_2': 8.0,
     'b_i_2': 7.289,
     'a_bs': 2.895}
    for name, (base, spread) in spreads.items():
        noise = np.random.default_rng([zlib.crc32(name.encode()), seed]).standard_normal(out[name].shape)
        drawn = base * np.exp(spread * noise) if base else spread * noise
        out[name] = __import__('jax').numpy.asarray(drawn.astype(out[name].dtype))
    for name, factor in factors.items():
        out[name] = (out[name] * factor).astype(out[name].dtype)
    return out
```

```python
import numpy as np
import concourse.bass as bass
from concourse import mybir
from contextlib import ExitStack

F32 = mybir.dt.float32
F32R = mybir.dt.float32r
ALU = mybir.AluOpType
ACT = mybir.ActivationFunctionType

P = 128
S = 256
D = 1024
KD = D // P
NR = S // P
TAPS = 31
PAD = TAPS - 1
TAPS2 = 4
DH = 64
HEADS = 8
KEEP = 64
NT = 4
FF = 4096
BW = 384
COPIES = P // (2 * HEADS)
NEG = -1e30
TAKEN = -3e38
EPS = 1e-6
LN_EPS = 1e-5
IDX_SCALE = (HEADS ** -0.5) * (DH ** -0.5)
UW = 2048
SLOTS = 3
LRU_C = 8.0

C_BIN, C_NORM, C_CONVB, C_GNG, C_GNB, C_PLE, C_FIN, C_MIX = 0, 64, 72, 80, 88, 96, 104, 112
D_MLP, D_CW2, D_CB2, D_BR, D_BI, D_LAM, D_LNG, D_LNB = 0, 8, 24, 28, 32, 36, 40, 48


def plan_units():
    units = []
    for j in range(4):
        units += [("ab", j), ("ag", j)]
    for kind, n in (("v", 4), ("u", 4), ("za", 4), ("zb", 4), ("ga", 4), ("gb", 4), ("pa", 4), ("pb", 4),
                    ("ple", 1), ("out", 4), ("ple2", 1), ("gate", 4), ("qi", 2), ("ki", 1), ("xc", 2),
                    ("yc", 2), ("kb", 2), ("qb", 2), ("vb", 2), ("qa", 2), ("ka", 2), ("va", 2),
                    ("g2", 12), ("pc2", 2), ("pb2", 2), ("pa2", 2), ("wo", 4), ("up", 1)):
        units += [(kind, j) for j in range(n)]
    for j in range(15):
        units += [("up", j + 1), ("down", j)]
    return units + [("down", 15)]


UNITS = plan_units()
FIRST = {}
for _c, (_kind, _j) in enumerate(UNITS):
    if _j == 0:
        FIRST[_kind] = _c
ACT_DRAINS = ("ab", "ag", "v", "u", "za", "zb", "ga", "gb", "up")
DVE_DRAINS = ("pa", "pb", "out", "gate", "qi", "ki", "xc", "yc", "kb", "qb", "vb", "qa", "ka", "va", "g2",
              "pc2", "pb2", "pa2", "wo")
TAPS_A_STEP = 9
GN_AT = 22
POOL_WORDS = 1024
SHARED_END = 64
IDX_AT = 54
TOP_AT = 58
LRU_AT = 58
HEAD_AT = 64
UP0 = FIRST["up"]
LOOP0 = UP0 + 1
LOOP_PAIRS = 15
PAIRS_A_TURN = 3


def shared(c):
    return c < SHARED_END and UNITS[c][0] not in ("ki", "ple", "ple2")


def pool_count(c):
    return sum(shared(b) for b in range(c + 1))


def drained_count(c):
    kinds = ACT_DRAINS if UNITS[c][0] in ACT_DRAINS else DVE_DRAINS
    return sum(k in kinds for k, _ in UNITS[:c + 1])


def block_program(nc, I, onehot, causal, scratch, out):
    ctx = ExitStack()
    with ctx:
        def sb(name, shape, dt=F32):
            return ctx.enter_context(nc.sbuf_tensor("s_" + name, shape, dt))

        def sem(name):
            return ctx.enter_context(nc.semaphore(name))

        raw = sb("raw", [P, SLOTS, UW])
        whi = sb("whi", [P, SLOTS, UW], F32R)
        wlo = sb("wlo", [P, SLOTS, UW], F32R)
        a_hi, a_lo = sb("a_hi", [P, KD, S], F32R), sb("a_lo", [P, KD, S], F32R)
        b_hi, b_lo = sb("b_hi", [P, KD, S], F32R), sb("b_lo", [P, KD, S], F32R)
        c_hi, c_lo = sb("c_hi", [P, NT, S], F32R), sb("c_lo", [P, NT, S], F32R)
        xT = sb("xT", [P, KD, S])
        abc = sb("abc", [P, 3 * UW])
        x_rows = abc[:, 0:UW].rearrange("p (r n) -> p r n", r=NR)
        v_rows = x_rows
        mix = abc[:, 0:UW].rearrange("p (t s) -> p t s", t=KD)
        gate_a = mix
        xn = abc[:, UW:2 * UW].rearrange("p (t s) -> p t s", t=KD)
        u_act = abc[:, UW:2 * UW].rearrange("p (t s) -> p t s", t=KD)
        gate_b = u_act
        conv = abc[:, 2 * UW:3 * UW].rearrange("p (t s) -> p t s", t=KD)
        sq1 = conv
        gates2 = abc[:, :].rearrange("p (t s) -> p t s", t=3 * KD)
        xcc = abc[:, 0:1024].rearrange("p (t s) -> p t s", t=NT)
        lru_r = abc[:, 1024:2048].rearrange("p (t s) -> p t s", t=NT)
        lru_i = abc[:, 2048:3072].rearrange("p (t s) -> p t s", t=NT)
        lru_a = abc[:, 3072:4096].rearrange("p (t s) -> p t s", t=NT)
        lru_b = abc[:, 4096:5120].rearrange("p (t s) -> p t s", t=NT)
        y_rows = abc[:, 0:UW].rearrange("p (r n) -> p r n", r=NR)
        y_sq = abc[:, UW:UW + D]
        reg_d = sb("reg_d", [P, KD * (S + PAD)])
        h_pad = reg_d[:, :].rearrange("p (t s) -> p t s", t=KD)
        sq2 = reg_d[:, 0:UW].rearrange("p (t s) -> p t s", t=KD)
        qi = reg_d[:, 0:1024].rearrange("p (t s) -> p t s", t=NT)
        ki = reg_d[:, 1024:1280]
        score = reg_d[:, 1280:1664]
        keep = reg_d[:, 1664:2048]
        z = [reg_d[:, 0:384], reg_d[:, 384:768]]
        reg_e = sb("reg_e", [P, UW])
        ws_rows = reg_e[:, 0:1024].rearrange("p (g j) -> p g j", g=KD)
        z_b = reg_e[:, :].rearrange("p (t s) -> p t s", t=KD)
        w_gates = reg_e[:, 0:1024].rearrange("p (w t m) -> p w t m", w=2, t=NT)
        causal_sb = reg_e[:, 1024:1408]
        onehot_sb = reg_e[0:32, 1408:1792]
        relb_sb = reg_e[0:32, 1792:1808]
        heads_sb = reg_e[0:32, 1808:1808 + P]
        qa = reg_e[:, 0:1024].rearrange("p (t s) -> p t s", t=NT)
        ka = reg_e[:, 1024:2048].rearrange("p (t s) -> p t s", t=NT)
        x4_rows = reg_e[:, :].rearrange("p (r n) -> p r n", r=NR)
        reg_f = sb("reg_f", [P, UW])
        bias_v = reg_f[0:1, 0:1024]
        p_rows = reg_f[:, 1024:1536].rearrange("p (r k) -> p r k", r=NR)
        merged = reg_f[:, :].rearrange("p (t s) -> p t s", t=KD)
        qb = reg_f[:, 0:1024].rearrange("p (t s) -> p t s", t=NT)
        kb = reg_f[:, 1024:2048].rearrange("p (t s) -> p t s", t=NT)
        relu_t = [reg_f[:, 0:384], reg_f[:, 384:768]]
        reg_w = sb("reg_w", [P, UW])
        wsT = reg_w[:, 0:1024].rearrange("p (g i) -> p g i", g=KD)
        gn_sq = reg_w[:, 0:1024].rearrange("p (t s) -> p t s", t=NT)
        bs_bc = reg_w[:, 1024:2048].rearrange("p (g i) -> p g i", g=KD)
        va = reg_w[:, 0:1024].rearrange("p (r n) -> p r n", r=NR)
        vb = reg_w[:, 1024:2048].rearrange("p (r n) -> p r n", r=NR)
        fin_bc = reg_w[:, 0:1024]
        tmp = sb("tmp", [P, 3, 2 * S])
        vec_rows = tmp[:, 0, :].rearrange("p (a b) -> p a b", a=4)
        reg_s = sb("reg_s", [P, 3476])
        yc = reg_s[:, 0:1024].rearrange("p (t s) -> p t s", t=NT)
        xc = reg_s[:, 1024:2060].rearrange("p (t s) -> p t s", t=NT)
        pT = [reg_s[:, 1024:1408], reg_s[:, 1408:1792]]
        bias_t = reg_s[:, 2060:3084].rearrange("p (b h s) -> p b h s", b=2, h=2)
        rv_sb = reg_s[:, 2060:2444]
        bkm = [reg_s[:, 3084:3468], reg_d[:, 768:1152]]
        ident = sb("ident", [P, P])
        ones = sb("ones", [P, P])
        o128 = sb("o128", [P, P])
        o1024 = sb("o1024", [P, P])
        sel_var = sb("sel_var", [P, NT, NT])
        sel_bc = sb("sel_bc", [NT, NT, P])
        vec = sb("vec", [P, 120])
        w_conv = sb("w_conv", [P, TAPS * KD])
        vec2 = sb("vec2", [P, 56])
        fm = sb("fm", [P, KD])
        r_bc = sb("r_bc", [P, S])
        r8_bc = sb("r8_bc", [P, S])
        r2_bc = sb("r2_bc", [P, S])
        r3_bc = sb("r3_bc", [P, S])
        r_col = sb("r_col", [P, NR])
        wi = sb("wi", [P, NR, HEADS])
        top8 = sb("top8", [P, NR, HEADS])
        ssq = sb("ssq", [P, NR])
        rinv = sb("rinv", [P, NR])
        rstd = sb("rstd", [P, NR])
        diag = tmp[:, 1, 0:S].rearrange("p (r n) -> p r n", r=NR)
        table_probe = sb("table_probe", [1, 1])
        bn = sb("bn", [P, NR, 4, 6])
        mv = sb("mv", [P, NR, 2])
        gs, gr = r2_bc[0:NT, :], r8_bc[0:NT, :]
        sp = sb("sp", [P, 8, NT])
        mx = sb("mx", [P, 16, NR])
        nmx = sb("nmx", [P, 16, NR])
        rs = sb("rs", [P, 16, NR])
        rr = sb("rr", [P, 16, NR])
        U = [ctx.enter_context(nc.psum_tensor(f"unit{i}", [P, 512], F32)) for i in range(SLOTS)]
        M = [ctx.enter_context(nc.psum_tensor(f"misc{i}", [P, 512], F32)) for i in range(5)]

        names = """loaded0 loaded1 loaded2 ki_loaded x_loaded0 x_loaded1 vec_loaded vec2_loaded early_loaded
            late_loaded consts hi_ready lo_ready multiplied act_drained dve_drained vchain achain
            ssq_ready rinv_ready rstd_ready diag_ready rbc_ready xn_ready vecs_T vecs_ready in_hi
            in_lo xT_raw xT_raw_ready pT_ready pT_hi pT_lo wsT_ready wsT_sb rowsum_mm bs_ready
            h_ready tap conv_mean d_ready gsq_ready gvar_ready gstd_ready grcp_ready gbc_ready
            hn_ready silu_ready yb_ready stats_v vvar_ready vstd_ready vn_ready mixed y_a ya_hi
            ya_lo yb_hi yb_lo mg_hi mg_lo x1_hi x1_lo sq_ready ms_ready r1_std gate_sig x2_ready
            b2_hi b2_lo sq12 ms2_ready s2_std s3_pre s3_std rb_ready rcol_T rcol_ready gfree dots
            relu_done sc_step bias_rows_T rv_ready heads_ready sq_summed y_mm pool_lo_ready scratch_stored
            bias_loaded0 bias_loaded1 xcc_ready ri_ready ri_act lru_act lru_dve yc_act g_act
            km_ready bkm_ready s_mm z_ready exp_done p_ready t_mm pT_copied pv_mm o_hi o_lo yc_hi
            yc_lo m2_hi m2_lo x4_hi x4_lo x4T x4_copied r4_ssq r4_ready sq_up h_hi h_lo fin_y
            fin_ssq fin_inv fin_std fin_out stored bias_reloaded0 bias_reloaded1 mg_added km_step
            mx_ready x3_ready u_gated mix_ready lam_abs lam_exp lam_ready""".split()
        sems = {n: sem(n) for n in names}
        loaded = [sems["loaded0"], sems["loaded1"], sems["loaded2"]]
        bias_loaded = [sems["bias_loaded0"], sems["bias_loaded1"]]
        bias_reloaded = [sems["bias_reloaded0"], sems["bias_reloaded1"]]
        Sm = sems

        block = ctx.enter_context(nc.Block())

        def unit_words(c):
            kind = UNITS[c][0]
            return {"ple": 1024, "ple2": 1024}.get(kind, UW)

        def ring_view(ring, c):
            kind = UNITS[c][0]
            if kind == "ki":
                return ring[:, c % SLOTS, :].rearrange("p (k n) -> p k n", k=KD)[:, :, 0:136]
            return ring[:, c % SLOTS, 0:unit_words(c)]

        off1 = {"u": 0, "v": 1024, "za": 2048, "ab": 3072, "ag": 4096, "zb": 5120, "ga": 6144, "gb": 7168}
        off2 = {"qa": 0, "ka": 512, "va": 1024, "qb": 1536, "kb": 2048, "vb": 2560, "qi": 3072, "ki": 3584,
                "wi": 3648, "xc": 3656, "yc": 4168, "g2": 4680}
        w1 = I["w_in"][0].rearrange("(k p) n -> p k n", p=P)
        w2 = I["w_in_2"][0].rearrange("(k p) n -> p k n", p=P)

        def unit_source(c):
            kind, j = UNITS[c]
            if kind in off1:
                return w1[:, :, off1[kind] + S * j:off1[kind] + S * (j + 1)]
            if kind in off2:
                return w2[:, :, off2[kind] + S * j:off2[kind] + S * (j + 1)]
            if kind in ("ple", "ple2"):
                h = 512 * (kind == "ple2")
                return I["w_ple"][0].rearrange("(k p) n -> p k n", p=P)[:, :, h:h + 512]
            if kind in ("pa2", "pb2", "pc2"):
                w = I["w_" + kind[:2] + "_2"][0].rearrange("(k p) n -> p k n", p=P)
                return w[:, :, 512 * j:512 * (j + 1)]
            w = I[{"pa": "w_pa", "pb": "w_pb", "out": "w_out", "gate": "w_ple_gate", "wo": "w_o_2",
                   "up": "w_up_2"}[kind]][0].rearrange("(k p) n -> p k n", p=P)
            return w[:, :, S * j:S * (j + 1)]

        w_up = I["w_up_2"][0].rearrange("(k p) n -> p k n", p=P)
        w_down = I["w_down_2"][0].rearrange("(j k p) n -> p j k n", p=P, k=2)

        def slot3(ring, slot, k):
            return ring[:, slot, :].rearrange("p (k n) -> p k n", k=k)

        def load_bias(eng, pair):
            head0 = HEADS + 2 * pair if pair < 4 else 2 * (pair - 4)
            src = bass.AP(tensor=scratch.tensor, offset=head0 * P * BW + P - 1,
                          ap=[[BW - 1, P], [P * BW, 2], [1, S]])
            done = bias_loaded[pair] if pair < 2 else bias_reloaded[pair % 2]
            eng.dma_start(bias_t[:, pair % 2, :, :], src).then_inc(done, 16)

        def wait_bias(eng, pair):
            if pair < 2:
                eng.wait_ge(bias_loaded[pair], 16)
            else:
                eng.wait_ge(bias_reloaded[pair % 2], 16 * (pair // 2))

        def rows(name):
            return I[name].rearrange("a (t p) -> (a t) p", p=P) if len(I[name].shape) == 2 else \
                I[name].rearrange("(t p) -> t p", p=P)

        vector_loads = [(0, C_BIN, rows("b_in")), (0, C_NORM, rows("norm_g")), (0, C_CONVB, rows("b_conv_b")),
                 (0, C_GNG, rows("b_gn_g")), (0, C_GNB, rows("b_gn_b")), (0, C_PLE, rows("ple_norm_g")),
                 (0, C_FIN, rows("final_g")), (0, C_MIX, rows("norm_mix_g_2"))]
        cw = I["b_conv_w"][0].rearrange("k (t p) -> (k t) p", p=P)
        vector_loads += [(1, 0, cw[0:P]), (2, 0, cw[P:TAPS * KD])]
        vector_loads += [(3, D_MLP, rows("norm_mlp_g_2")),
                  (3, D_CW2, I["conv_w_2"][0].rearrange("k (t p) -> (k t) p", p=P)),
                  (3, D_CB2, rows("conv_b_2")), (3, D_BR, rows("b_r_2")), (3, D_BI, rows("b_i_2")),
                  (3, D_LAM, rows("lru_lambda_2")), (3, D_LNG, rows("a_ln_g")), (3, D_LNB, rows("a_ln_b"))]
        @block.sync
        def _(sy):
            for r in range(NR):
                sy.dma_start(x_rows[:, r, :], I["x"][0].rearrange("(r p) d -> r p d", p=P)[r]
                             ).then_inc(Sm[f"x_loaded{r}"], 16)

            def load(c):
                if c >= SLOTS:
                    sy.wait_ge(Sm["lo_ready"], c - SLOTS + 1)
                    if shared(c - SLOTS):
                        sy.wait_ge(Sm["pool_lo_ready"], pool_count(c - SLOTS))
                kind, j = UNITS[c]
                k = {"ple": 2, "ple2": 2, "pa2": 4, "pb2": 4, "pc2": 4}.get(kind, KD)
                if kind == "ki":
                    dst = slot3(raw, c % SLOTS, KD)
                    for half in range(2):
                        sy.dma_start(dst[:, :, 64 * half:64 * half + 64],
                                     w2[:, :, off2["ki"]:off2["ki"] + 64]).then_inc(Sm["ki_loaded"], 16)
                    sy.dma_start(dst[:, :, 128:136],
                                 w2[:, :, off2["wi"]:off2["wi"] + 8]).then_inc(loaded[c % SLOTS], 16)
                    return
                dst = raw[:, c % SLOTS, 0:unit_words(c)].rearrange("p (k n) -> p k n", k=k)
                sy.dma_start(dst, unit_source(c)).then_inc(loaded[c % SLOTS], 16)

            for c in range(LOOP0):
                load(c)
                if c == 0:
                    for tile, r0, src in vector_loads:
                        sy.dma_start(vec_rows[r0:r0 + src.shape[0], tile, :], src
                                     ).then_inc(Sm["vec2_loaded" if tile else "vec_loaded"], 16)
                if c == 1:
                    sy.dma_start(ws_rows, I["a_ws"][0].rearrange("g i j -> i g j")).then_inc(Sm["early_loaded"], 16)
                    sy.dma_start(bs_bc, I["a_bs"][0].partition_broadcast(P)).then_inc(Sm["early_loaded"], 16)
                    sy.dma_start(bias_v, I["b_in"][:, 1024:2048]).then_inc(Sm["early_loaded"], 16)
                    sy.dma_start(p_rows, I["p"][0, 0].rearrange("(r p) k -> p r k", p=P)
                                 ).then_inc(Sm["early_loaded"], 16)
                if c == FIRST["pb"] + 1:
                    sy.wait_ge(Sm["yb_ready"], 4)
                    sy.dma_start(causal_sb, causal).then_inc(Sm["late_loaded"], 16)
                    sy.dma_start(onehot_sb, onehot).then_inc(Sm["late_loaded"], 16)
                    sy.dma_start(relb_sb, I["rel_bias_2"]).then_inc(Sm["late_loaded"], 16)
                    sy.wait_ge(Sm["gfree"], 1)
                    for w, name in enumerate(("w_r_2", "w_i_2")):
                        for half in range(2):
                            sy.dma_start(w_gates[64 * half:64 * half + 64, w, :, 64 * half:64 * half + 64],
                                         I[name][0].rearrange("(t h) c d -> h c t d", h=2)[half]
                                         ).then_inc(Sm["late_loaded"], 16)
                if c == FIRST["wo"]:
                    sy.wait_ge(Sm["pv_mm"], 2 * HEADS)
                    sy.dma_start(fin_bc, I["final_norm_g_2"].partition_broadcast(P)).then_inc(Sm["late_loaded"], 16)
                if c == FIRST["gate"]:
                    sy.wait_ge(Sm["rv_ready"], 2)
                    sy.dma_start(scratch, rv_sb.rearrange("p (a u) -> p a u", a=1).to_broadcast([P, P // COPIES, BW])
                                 ).then_inc(Sm["scratch_stored"], 16)
                    sy.wait_ge(Sm["scratch_stored"], 16)
                if c == FIRST["gate"] + 1:
                    load_bias(sy, 0)
                    load_bias(sy, 1)
            with sy.Fori(0, LOOP_PAIRS // PAIRS_A_TURN) as i:
                for q in range(PAIRS_A_TURN):
                    for half in range(2):
                        c = LOOP0 + 2 * q + half
                        sy.wait_ge(Sm["lo_ready"], 6 * i + (c - SLOTS + 1))
                        if half == 0:
                            src = w_up[:, :, bass.ds(S * PAIRS_A_TURN * i + S * (q + 1), S)]
                            dst = slot3(raw, c % SLOTS, KD)
                        else:
                            src = w_down[:, bass.ds(PAIRS_A_TURN * i + q, 1), :, :].rearrange("p a k n -> p (a k) n")
                            dst = slot3(raw, c % SLOTS, 2)
                        sy.dma_start(dst, src).then_inc(loaded[c % SLOTS], 16)
            c = LOOP0 + 2 * LOOP_PAIRS
            sy.wait_ge(Sm["lo_ready"], c - SLOTS + 1)
            sy.dma_start(slot3(raw, c % SLOTS, 2), w_down[:, FF // S - 1, :, :]).then_inc(loaded[c % SLOTS], 16)
            for n in range(2 * NR):
                r, cols = n // 2, slice(512 * (n % 2), 512 * (n % 2) + 512)
                sy.wait_ge(Sm["fin_out"], n + 1)
                sy.dma_start(out[0].rearrange("(r p) d -> r p d", p=P)[r][:, cols], y_rows[:, r, cols]
                             ).then_inc(Sm["stored"], 16)
            sy.wait_ge(Sm["stored"], 16 * 2 * NR)

        @block.gpsimd
        def _(gp):
            for t, val in ((ident, 0.0), (ones, 1.0), (o128, 1.0 / P), (o1024, 1.0 / D)):
                gp.memset(t[:, :], val).then_inc(Sm["consts"], 1)
            gp.memset(sel_var[:, :, :], 0.0).then_inc(Sm["consts"], 1)
            gp.memset(sel_bc[:, :, :], 0.0).then_inc(Sm["consts"], 1)
            gp.wait_ge(Sm["consts"], 6)
            gp.affine_select(out=ident[:, :], in_=ident[:, :], compare_op=ALU.not_equal, fill=1.0, base=0,
                             pattern=[[-1, P]], channel_multiplier=1).then_inc(Sm["consts"], 1)
            gp.affine_select(out=sel_var[:, :, :], in_=sel_var[:, :, :], compare_op=ALU.not_equal, fill=1.0 / P,
                             base=0, pattern=[[1, NT], [-1, NT]], channel_multiplier=0).then_inc(Sm["consts"], 1)
            gp.affine_select(out=sel_bc[:, :, :], in_=sel_bc[:, :, :], compare_op=ALU.not_equal, fill=1.0, base=0,
                             pattern=[[-1, NT], [0, P]], channel_multiplier=1).then_inc(Sm["consts"], 1)
            gp.memset(h_pad[:, :, 0:PAD], 0.0).then_inc(Sm["h_ready"], 1)
            for c in range(SHARED_END):
                if c == FIRST["pa"] + 4:
                    gp.wait_ge(Sm["yb_ready"], 4)
                    gp.memset(w_gates, 0.0).then_inc(Sm["gfree"], 1)
                if shared(c):
                    cols = slice(UW - POOL_WORDS, UW)
                    gp.wait_ge(Sm["hi_ready"], c + 1)
                    gp.tensor_tensor(wlo[:, c % SLOTS, cols], raw[:, c % SLOTS, cols],
                                     whi[:, c % SLOTS, cols].bitcast(F32), ALU.subtract
                                     ).then_inc(Sm["pool_lo_ready"], 1)
                if FIRST["out"] + 2 < c <= FIRST["out"] + 5:
                    n = c - FIRST["out"] - 2
                    gp.wait_ge(Sm["sq_ready"], n + 1)
                    if n > 1:
                        gp.wait_ge(Sm["sq_summed"], n - 1)
                    gp.tensor_tensor(sq1[:, 0:2, :], sq1[:, 0:2, :], sq1[:, 2 * n:2 * n + 2, :], ALU.add
                                     ).then_inc(Sm["sq_summed"], 1)
                if c < 2:
                    continue
                kind, j = UNITS[c - 2]
                if kind == "ag":
                    gp.wait_ge(Sm["act_drained"], c - 1)
                    a, g = (2 * j) % 3, (2 * j + 1) % 3
                    gp.tensor_tensor(h_pad[:, 2 * j:2 * j + 2, PAD:PAD + S],
                                     tmp[:, a, :].rearrange("p (t s) -> p t s", t=2),
                                     tmp[:, g, :].rearrange("p (t s) -> p t s", t=2), ALU.mult
                                     ).then_inc(Sm["h_ready"], 1)
                elif kind == "za":
                    gp.wait_ge(Sm["act_drained"], c - 1)
                    gp.tensor_tensor(u_act[:, 2 * j:2 * j + 2, :], u_act[:, 2 * j:2 * j + 2, :],
                                     tmp[:, (8 + j) % 3, :].rearrange("p (t s) -> p t s", t=2), ALU.mult
                                     ).then_inc(Sm["u_gated"], 1)
            gp.wait_ge(Sm["km_ready"], 2)
            for h in range(HEADS):
                wait_bias(gp, h // 2)
                if h >= 2:
                    gp.wait_ge(Sm["z_ready"], h - 1)
                bt = bias_t[:, (h // 2) % 2, h % 2, :]
                gp.tensor_tensor(bkm[h % 2][:, 0:S], bt, keep[:, 0:S], ALU.add).then_inc(Sm["bkm_ready"], 1)
                gp.tensor_tensor(bkm[h % 2][:, S:S + P], bt[:, P:S], keep[:, S:S + P], ALU.add
                                 ).then_inc(Sm["bkm_ready"], 1)
                if h % 2:
                    pair = h // 2 + 2
                    gp.wait_ge(Sm["bkm_ready"], 2 * (h + 1))
                    load_bias(gp, pair)
            for pair in range(6, 8):
                gp.wait_ge(Sm["z_ready"], 2 * (pair - 1))
                load_bias(gp, pair)

        @block.scalar
        def _(act):
            chain = [0]

            def link(ins):
                chain[0] += 1
                ins.then_inc(Sm["achain"], 1)
                act.wait_ge(Sm["achain"], chain[0])

            act.wait_ge(Sm["consts"], 9)
            act.activation(table_probe[:, :], ones[0:1, 0:1], ACT.Sqrt)

            def hi(c):
                act.wait_ge(loaded[c % SLOTS], 16 * (c // SLOTS + 1))
                if UNITS[c][0] == "ki":
                    act.wait_ge(Sm["ki_loaded"], 32)
                if c >= SLOTS:
                    act.wait_ge(Sm["multiplied"], c - SLOTS + 1)
                act.activation(ring_view(whi, c), ring_view(raw, c), ACT.Copy).then_inc(Sm["hi_ready"], 1)

            for r in range(NR):
                act.wait_ge(Sm[f"x_loaded{r}"], 16)
                act.activation(abc[:, 2 * UW + D * r:2 * UW + D * (r + 1)], x_rows[:, r, :], ACT.Square,
                               accum_out=ssq[:, r:r + 1]).then_inc(Sm["ssq_ready"], 1)
            act.wait_ge(Sm["rinv_ready"], 1)
            act.activation(rstd[:, :], rinv[:, :], ACT.Sqrt).then_inc(Sm["rstd_ready"], 1)
            hi(0)
            for k in range(KD):
                act.wait_ge(Sm["xn_ready"], k + 1)
                act.activation(a_hi[:, k, :], xn[:, k, :], ACT.Copy).then_inc(Sm["in_hi"], 1)
            hi(1)

            def drain_tiles(c, dst, func, col):
                act.wait_ge(Sm["multiplied"], c + 1)
                for n in range(2):
                    ins = act.activation(dst(n), U[c % SLOTS][:, S * n:S * n + S], func,
                                         bias=vec[:, col + n:col + n + 1])
                ins.then_inc(Sm["act_drained"], 1)

            def tmp_tile(slot):
                return lambda n: tmp[:, slot, S * n:S * n + S]

            tmp_use = [0]

            def take_tmp():
                n = tmp_use[0]
                tmp_use[0] += 1
                if 3 <= n < 11:
                    act.wait_ge(Sm["h_ready"], (n - 3) // 2 + 2)
                elif n >= 11:
                    act.wait_ge(Sm["u_gated"], n - 10)
                return n % 3

            def gn_square(b):
                act.wait_ge(Sm["d_ready"], 2 * (b + 1))
                act.activation(gn_sq, conv[:, 4 * b:4 * b + 4, :], ACT.Square).then_inc(Sm["gsq_ready"], 1)

            def gn_std(b):
                act.wait_ge(Sm["gvar_ready"], b + 1)
                act.activation(gs, M[2][0:NT, 0:S], ACT.Sqrt, bias=LN_EPS).then_inc(Sm["gstd_ready"], 1)

            def gn_silu(b):
                act.wait_ge(Sm["hn_ready"], 2 * (b + 1))
                for t in range(4 * b, 4 * b + 4):
                    act.activation(conv[:, t, :], conv[:, t, :], ACT.Silu, bias=vec[:, C_GNB + t:C_GNB + t + 1],
                                   scale=vec[:, C_GNG + t:C_GNG + t + 1]).then_inc(Sm["silu_ready"], 1)

            for c in range(1, FIRST["pa"] + 1):
                kind, j = UNITS[c - 1]
                col = C_BIN + off1[kind] // P + 2 * j
                hi(c + 1)
                if c == 1:
                    act.wait_ge(Sm["vecs_ready"], 4)
                if kind == "ab":
                    drain_tiles(c - 1, tmp_tile(take_tmp()), ACT.Identity, col)
                elif kind == "ag":
                    drain_tiles(c - 1, tmp_tile(take_tmp()), ACT.Sigmoid, col)
                elif kind == "v":
                    act.wait_ge(Sm["multiplied"], c)
                    if j == 0:
                        act.wait_ge(Sm["xT_raw"], 4)
                    act.activation(v_rows[:, :, S * j:S * j + S],
                                   U[(c - 1) % SLOTS][:, :].rearrange("p (r s) -> p r s", r=NR),
                                   ACT.Gelu_apprx_tanh).then_inc(Sm["act_drained"], 1)
                elif kind == "u":
                    drain_tiles(c - 1, lambda n, j=j: u_act[:, 2 * j + n, :], ACT.Gelu_apprx_tanh, col)
                elif kind == "za":
                    drain_tiles(c - 1, tmp_tile(take_tmp()), ACT.Silu, col)
                elif kind == "zb":
                    if j == 0:
                        act.wait_ge(Sm["wsT_ready"], 2)
                    drain_tiles(c - 1, lambda n, j=j: z_b[:, 2 * j + n, :], ACT.Silu, col)
                elif kind == "ga":
                    act.wait_ge(Sm["ya_lo"], j + 1)
                    drain_tiles(c - 1, lambda n, j=j: gate_a[:, 2 * j + n, :], ACT.Sigmoid, col)
                elif kind == "gb":
                    act.wait_ge(Sm["y_a"], j + 1)
                    drain_tiles(c - 1, lambda n, j=j: gate_b[:, 2 * j + n, :], ACT.Sigmoid, col)
                if c == 2:
                    act.wait_ge(Sm["pT_ready"], 1)
                    act.activation(c_hi[:, 0:2, :], M[4][:, :].rearrange("p (k s) -> p k s", k=2), ACT.Copy
                                   ).then_inc(Sm["pT_hi"], 1)
                if c == 7:
                    for h in range(2):
                        act.wait_ge(Sm["wsT_ready"], h + 1)
                        ins = act.activation(wsT[:, 4 * h:4 * h + 4, :],
                                             M[h][:, :].rearrange("p (g i) -> p g i", g=4), ACT.Copy)
                        ins.then_inc(Sm["wsT_sb"], 1)
                if c == FIRST["u"] + 1:
                    act.wait_ge(Sm["vvar_ready"], 1)
                    act.activation(rstd[:, :], rinv[:, :], ACT.Sqrt).then_inc(Sm["vstd_ready"], 1)
                if kind == "zb":
                    act.wait_ge(Sm["y_a"], j + 1)
                    act.activation(b_hi[:, 2 * j:2 * j + 2, :], mix[:, 2 * j:2 * j + 2, :], ACT.Copy
                                   ).then_inc(Sm["ya_hi"], 1)
                if c == GN_AT + 1:
                    gn_square(0)
                if c == GN_AT + 2:
                    gn_std(0)
                if c == GN_AT + 6:
                    gn_silu(0)
            c = FIRST["pa"]
            hi(c + 2)
            gn_square(1)
            hi(c + 3)
            gn_std(1)
            hi(c + 4)
            gn_silu(1)
            act.wait_ge(Sm["multiplied"], FIRST["pa"])
            for b in range(2):
                act.wait_ge(Sm["yb_ready"], 2 * (b + 1))
                act.activation(a_hi[:, 4 * b:4 * b + 4, :], conv[:, 4 * b:4 * b + 4, :], ACT.Copy
                               ).then_inc(Sm["yb_hi"], 1)
            hi(c + 5)
            for j in range(4):
                hi(FIRST["pb"] + 2 + j)
                act.wait_ge(Sm["mg_added"], j + 1)
                act.activation(b_hi[:, 2 * j:2 * j + 2, :], merged[:, 2 * j:2 * j + 2, :], ACT.Copy
                               ).then_inc(Sm["mg_hi"], 1)
            hi(FIRST["out"] + 1)
            for j in range(4):
                c = FIRST["out"] + j
                hi(c + 2)
                act.wait_ge(Sm["dve_drained"], drained_count(c))
                for k in (2 * j, 2 * j + 1):
                    act.activation(a_hi[:, k, :], xT[:, k, :], ACT.Copy, scale=vec[:, C_PLE + k:C_PLE + k + 1]
                                   ).then_inc(Sm["x1_hi"], 1)
                act.activation(sq1[:, 2 * j:2 * j + 2, :], xT[:, 2 * j:2 * j + 2, :], ACT.Square
                               ).then_inc(Sm["sq_ready"], 1)
            act.wait_ge(Sm["lam_abs"], 1)
            act.activation(sp[:, 1, :], sp[:, 0, :], ACT.Exp, scale=-1.0).then_inc(Sm["lam_exp"], 1)
            hi(FIRST["gate"] + 1)
            act.wait_ge(Sm["ms_ready"], 1)
            act.activation(r3_bc[:, :], M[4][:, 0:S], ACT.Sqrt, bias=EPS).then_inc(Sm["r1_std"], 1)
            for j in range(4):
                c = FIRST["gate"] + j
                act.wait_ge(Sm["dve_drained"], drained_count(c))
                act.activation(tmp[:, j % 3, :], tmp[:, j % 3, :], ACT.Sigmoid).then_inc(Sm["gate_sig"], 1)
                if j < 3:
                    hi(c + 2)
                act.wait_ge(Sm["x2_ready"], j + 1)
                for k in (2 * j, 2 * j + 1):
                    act.activation(b_hi[:, k, :], xT[:, k, :], ACT.Copy, scale=fm[:, k:k + 1]
                                   ).then_inc(Sm["b2_hi"], 1)
                act.activation(sq1[:, 2 * j:2 * j + 2, :], xT[:, 2 * j:2 * j + 2, :], ACT.Square)
                for k in (2 * j, 2 * j + 1):
                    ins = act.activation(sq2[:, k, :], xT[:, k, :], ACT.Square, scale=vec[:, C_FIN + k:C_FIN + k + 1])
                ins.then_inc(Sm["sq12"], 1)
            hi(FIRST["qi"] + 1)
            hi(FIRST["qi"] + 2)
            act.wait_ge(Sm["ms2_ready"], 1)
            act.activation(r3_bc[:, :], M[4][:, 0:S], ACT.Sqrt, bias=EPS).then_inc(Sm["s2_std"], 1)
            act.wait_ge(Sm["s3_pre"], 1)
            act.activation(r3_bc[:, :], r8_bc[:, :], ACT.Sqrt, bias=EPS).then_inc(Sm["s3_std"], 1)

            def relus(h):
                act.wait_ge(Sm["dots"], h + 1)
                if h >= 2:
                    act.wait_ge(Sm["sc_step"], 2 * (h - 1))
                act.activation(relu_t[h % 2], M[h % 4][:, 0:384], ACT.Relu).then_inc(Sm["relu_done"], 1)

            def exps(h):
                act.wait_ge(Sm["z_ready"], h + 1)
                for r, cols in ((1, slice(0, S)), (0, slice(S, S + P))):
                    act.activation(z[h % 2][:, cols], z[h % 2][:, cols], ACT.Exp, bias=nmx[:, h, r:r + 1],
                                   accum_out=rs[:, h, r:r + 1]).then_inc(Sm["exp_done"], 1)

            def copy_pT(h):
                act.wait_ge(Sm["t_mm"], h + 1)
                if h >= 2:
                    act.wait_ge(Sm["pv_mm"], h - 1)
                act.activation(pT[h % 2], M[2 + h % 2][:, 0:384], ACT.Copy).then_inc(Sm["pT_copied"], 1)

            def round_o(h):
                if h % 2:
                    act.wait_ge(Sm["pv_mm"], h + 1)
                    t = h // 2
                    act.activation(a_hi[:, t, :], M[4][:, S * (t % 2):S * (t % 2) + S], ACT.Copy
                                   ).then_inc(Sm["o_hi"], 1)

            for c in range(FIRST["qi"] + 1, FIRST["pc2"] + 1):
                kind, j = UNITS[c - 1]
                hi(c + 2)
                if kind == "yc":
                    act.wait_ge(Sm["dve_drained"], drained_count(c - 1))
                    act.activation(yc[:, 2 * j:2 * j + 2, :], tmp[:, j, :].rearrange("p (t s) -> p t s", t=2),
                                   ACT.Gelu_apprx_tanh).then_inc(Sm["yc_act"], 1)
                if IDX_AT < c <= IDX_AT + 4:
                    for h in (2 * (c - IDX_AT - 1), 2 * (c - IDX_AT - 1) + 1):
                        relus(h)
                if c == LRU_AT + 1:
                    for t in range(NT):
                        act.wait_ge(Sm["ri_ready"], t + 1)
                        act.activation(lru_r[:, t, :], M[t][:, 0:S], ACT.Sigmoid, bias=vec2[:, D_BR + t:D_BR + t + 1])
                        act.activation(lru_i[:, t, :], M[t][:, S:2 * S], ACT.Sigmoid,
                                       bias=vec2[:, D_BI + t:D_BI + t + 1]).then_inc(Sm["ri_act"], 1)
                if c == LRU_AT + 2:
                    for t in range(NT):
                        col = sp[:, 7, t:t + 1]
                        if t == 0:
                            act.wait_ge(Sm["ri_act"], NT)
                            act.wait_ge(Sm["lam_ready"], 1)
                        act.activation(lru_a[:, t, :], lru_r[:, t, :], ACT.Exp, scale=col)
                        act.activation(lru_b[:, t, :], lru_r[:, t, :], ACT.Tanh, scale=col
                                       ).then_inc(Sm["lru_act"], 1)
                if c == LRU_AT + 3:
                    act.wait_ge(Sm["lru_dve"], 1)
                    act.activation(lru_b, lru_b, ACT.Sqrt, scale=-1.0).then_inc(Sm["lru_act"], 1)
                if c == LRU_AT + 5:
                    act.wait_ge(Sm["lru_dve"], 4)
                    act.activation(c_hi[:, :, :], lru_a, ACT.Copy).then_inc(Sm["yc_hi"], 1)
                if kind == "g2":
                    act.wait_ge(Sm["dve_drained"], drained_count(c - 1))
                    if j == 0:
                        act.wait_ge(Sm["yc_lo"], 1)
                    act.activation(gates2[:, 2 * j:2 * j + 2, :],
                                   tmp[:, j % 3, :].rearrange("p (t s) -> p t s", t=2), ACT.Tanh, scale=0.5
                                   ).then_inc(Sm["g_act"], 1)
                h = c - HEAD_AT
                if 0 <= h < 16:
                    exps(h)
                if 1 <= h < 17:
                    copy_pT(h - 1)
                if 2 <= h < 18:
                    round_o(h - 2)
            for j in range(6):
                if j < 4:
                    hi(FIRST["pc2"] + 3 + j)
                if j >= 4:
                    for half in range(2):
                        n = 2 * (j - 4) + half
                        act.wait_ge(Sm["mg_added"], 4 + n + 1)
                        act.activation(b_hi[:, 2 * n:2 * n + 2, :], merged[:, 2 * n:2 * n + 2, :], ACT.Copy,
                                       scale=0.5).then_inc(Sm["m2_hi"], 1)
                    hi(FIRST["pc2"] + 3 + j)
            for j in range(4):
                c = FIRST["wo"] + j
                act.wait_ge(Sm["dve_drained"], drained_count(c))
                for k in (2 * j, 2 * j + 1):
                    act.activation(a_hi[:, k, :], xT[:, k, :], ACT.Copy, scale=vec2[:, D_MLP + k:D_MLP + k + 1]
                                   ).then_inc(Sm["x4_hi"], 1)
                hi(c + 3)
            for b in range(4):
                act.wait_ge(Sm["x4T"], b + 1)
                act.activation(x4_rows[:, :, S * b:S * b + S].rearrange("p r (k s) -> p k r s", k=2),
                               M[b][:, :].rearrange("p (k r s) -> p k r s", k=2, r=NR), ACT.Copy
                               ).then_inc(Sm["x4_copied"], 1)
            act.wait_ge(Sm["x4_copied"], 4)
            for r in range(NR):
                act.activation(y_sq, x4_rows[:, r, :], ACT.Square, accum_out=ssq[:, r:r + 1]
                               ).then_inc(Sm["r4_ssq"], 1)
                act.wait_ge(Sm["r4_ssq"], r + 1)

            act.wait_ge(Sm["multiplied"], UP0 + 1)
            act.activation(tmp[:, 0, :], U[UP0 % SLOTS][:, :], ACT.Relu).then_inc(Sm["act_drained"], 1)
            act.wait_ge(Sm["sq_up"], 1)
            act.activation(b_hi[:, 0:2, :], tmp[:, 1, :].rearrange("p (t s) -> p t s", t=2), ACT.Copy
                           ).then_inc(Sm["h_hi"], 1)

            def hi_at(slot, count_loaded, count_mult):
                act.wait_ge(loaded[slot], count_loaded)
                act.wait_ge(Sm["multiplied"], count_mult)
                act.activation(whi[:, slot, :], raw[:, slot, :], ACT.Copy).then_inc(Sm["hi_ready"], 1)

            def loop_body(i, last=False):
                for q in range(PAIRS_A_TURN):
                    for half in range(2):
                        c = LOOP0 + 2 * q + half
                        n = c + 2
                        if not (last and n > LOOP0 + 6):
                            hi_at(n % SLOTS, 32 * i + 16 * (n // SLOTS + 1), 6 * i + (n - SLOTS + 1))
                        if half == 1:
                            act.wait_ge(Sm["multiplied"], 6 * i + c)
                            act.wait_ge(Sm["h_lo"], 3 * i + q + 1)
                            act.activation(tmp[:, 0, :], U[(c - 1) % SLOTS][:, :], ACT.Relu
                                           ).then_inc(Sm["act_drained"], 1)
                            act.wait_ge(Sm["sq_up"], 3 * i + q + 2)
                            b = 2 * ((q + 1) % 3)
                            act.activation(b_hi[:, b:b + 2, :], tmp[:, 1, :].rearrange("p (t s) -> p t s", t=2),
                                           ACT.Copy).then_inc(Sm["h_hi"], 1)

            with act.Fori(0, LOOP_PAIRS // PAIRS_A_TURN - 1) as i:
                loop_body(i)
            loop_body(LOOP_PAIRS // PAIRS_A_TURN - 1, last=True)
            act.activation(table_probe[:, :], ones[0:1, 0:1], ACT.Sqrt)
            for r in range(NR):
                act.wait_ge(Sm["fin_y"], r + 1)
                act.activation(y_sq, y_rows[:, r, :], ACT.Square, accum_out=ssq[:, r:r + 1]
                               ).then_inc(Sm["fin_ssq"], 1)
                act.wait_ge(Sm["fin_inv"], r + 1)
                act.activation(rstd[:, r:r + 1], rinv[:, r:r + 1], ACT.Sqrt).then_inc(Sm["fin_std"], 1)

        @block.vector
        def _(ve):
            chain = [0]

            def link(ins):
                chain[0] += 1
                ins.then_inc(Sm["vchain"], 1)
                ve.wait_ge(Sm["vchain"], chain[0])

            def col(t, n):
                return t[:, n:n + 1]

            def lo(c):
                ve.wait_ge(Sm["hi_ready"], c + 1)
                dst, src, part = ring_view(wlo, c), ring_view(raw, c), ring_view(whi, c)
                if shared(c):
                    dst, src, part = (ap[:, 0:UW - POOL_WORDS] for ap in (dst, src, part))
                ve.tensor_tensor(dst, src, part.bitcast(F32), ALU.subtract).then_inc(Sm["lo_ready"], 1)

            def split_lo(dst, src, part, done):
                ve.tensor_tensor(dst, src, part.bitcast(F32), ALU.subtract).then_inc(Sm[done], 1)

            def two(ap):
                return ap.rearrange("p (t s) -> p t s", t=2)

            ve.wait_ge(Sm["ssq_ready"], NR)
            link(ve.tensor_scalar(rinv[:, :], ssq[:, :], 1.0 / D, EPS, ALU.mult, ALU.add))
            ve.reciprocal(rinv[:, :], rinv[:, :]).then_inc(Sm["rinv_ready"], 1)
            ve.wait_ge(Sm["consts"], 9)
            ve.wait_ge(Sm["rstd_ready"], 1)
            for r in range(NR):
                ve.tensor_scalar(diag[:, r, :], ident[:, :], rstd[:, r:r + 1], None, ALU.mult
                                 ).then_inc(Sm["diag_ready"], 1)
            ve.wait_ge(Sm["rbc_ready"], 1)
            link(ve.tensor_copy(r_bc[:, :], U[2][:, 0:S]))
            ve.wait_ge(Sm["vecs_T"], 1)
            ve.tensor_copy(vec[:, :], M[4][:, 0:120]).then_inc(Sm["vecs_ready"], 1)
            ve.wait_ge(Sm["vecs_ready"], 1)
            for k in range(KD + 2):
                if k == 2:
                    lo(0)
                if k < KD:
                    ve.wait_ge(Sm["xT_raw"], k // 2 + 1)
                    ve.scalar_tensor_tensor(xn[:, k, :], M[k // 2][:, S * (k % 2):S * (k % 2) + S],
                                            col(vec, C_NORM + k), r_bc[:, :], ALU.mult, ALU.mult
                                            ).then_inc(Sm["xn_ready"], 1)
                if k >= 2:
                    ve.wait_ge(Sm["in_hi"], k - 1)
                    split_lo(a_lo[:, k - 2, :], xn[:, k - 2, :], a_hi[:, k - 2, :], "in_lo")
            ve.wait_ge(Sm["vecs_T"], 4)
            ve.tensor_copy(w_conv[:, 0:P], M[4][:, 128:256]).then_inc(Sm["vecs_ready"], 1)
            ve.tensor_copy(w_conv[:, P:TAPS * KD], M[4][:, 256:376]).then_inc(Sm["vecs_ready"], 1)
            ve.tensor_copy(vec2[:, :], M[4][:, 384:440]).then_inc(Sm["vecs_ready"], 1)
            ve.wait_ge(Sm["vecs_ready"], 4)
            lo(1)
            link(ve.tensor_tensor(fm[:, :], vec[:, C_FIN:C_FIN + KD], vec[:, C_MIX:C_MIX + KD], ALU.mult))

            taps = [0]

            def conv_taps(n):
                for _ in range(n):
                    i = taps[0]
                    if i >= TAPS * KD:
                        return
                    taps[0] += 1
                    pair, k, t = i // (2 * TAPS), (i % (2 * TAPS)) // 2, 2 * (i // (2 * TAPS)) + i % 2
                    if k == 0:
                        ve.wait_ge(Sm["h_ready"], pair + 2)
                        ve.tensor_scalar(conv[:, t, :], h_pad[:, t, 0:S], col(w_conv, t), col(vec, C_CONVB + t),
                                         ALU.mult, ALU.add).then_inc(Sm["tap"], 1)
                    else:
                        ve.wait_ge(Sm["tap"], i - 1)
                        ve.scalar_tensor_tensor(conv[:, t, :], h_pad[:, t, k:k + S], col(w_conv, k * KD + t),
                                                conv[:, t, :], ALU.mult, ALU.add).then_inc(Sm["tap"], 1)

            def gn_center(b):
                for h in range(2):
                    ve.wait_ge(Sm["conv_mean"], 2 * b + h + 1)
                    tiles = conv[:, 4 * b + 2 * h:4 * b + 2 * h + 2, :]
                    ve.tensor_tensor(tiles, tiles, two(M[h][:, :]), ALU.subtract).then_inc(Sm["d_ready"], 1)

            def gn_recip(b):
                ve.wait_ge(Sm["gstd_ready"], b + 1)
                ve.reciprocal(gr, gs).then_inc(Sm["grcp_ready"], 1)

            def gn_scale(b):
                for h in range(2):
                    ve.wait_ge(Sm["gbc_ready"], 2 * b + h + 1)
                    tiles = conv[:, 4 * b + 2 * h:4 * b + 2 * h + 2, :]
                    ve.tensor_tensor(tiles, tiles, two(M[h][:, :]), ALU.mult).then_inc(Sm["hn_ready"], 1)

            def y_b(b):
                for h in range(2):
                    t = 4 * b + 2 * h
                    ve.wait_ge(Sm["silu_ready"], t + 2)
                    ve.wait_ge(Sm["act_drained"], drained_count(FIRST["zb"] + t // 2))
                    ve.tensor_tensor(conv[:, t:t + 2, :], conv[:, t:t + 2, :], z_b[:, t:t + 2, :], ALU.mult
                                     ).then_inc(Sm["yb_ready"], 1)

            for c in range(1, FIRST["pa"] + 1):
                kind, j = UNITS[c - 1]
                lo(c + 1)
                if kind == "v":
                    ve.wait_ge(Sm["act_drained"], c)
                    for r in range(NR):
                        ve.bn_stats(bn[:, r, j, :], v_rows[:, r, S * j:S * j + S]).then_inc(Sm["stats_v"], 1)
                if c == 2:
                    ve.wait_ge(Sm["pT_hi"], 1)
                    split_lo(c_lo[:, 0:2, :], two(M[4][:, :]), c_hi[:, 0:2, :], "pT_lo")
                if c == 4:
                    for b in range(4):
                        ve.wait_ge(Sm["xT_raw"], b + 1)
                        ve.tensor_copy(xT[:, 2 * b:2 * b + 2, :], two(M[b][:, :])).then_inc(Sm["xT_raw_ready"], 1)
                if c == 8:
                    ve.wait_ge(Sm["wsT_sb"], 2)
                    ve.memset(wsT[64:P, :, 0:64], 0.0).then_inc(Sm["wsT_sb"], 1)
                if c == 10:
                    for g in range(KD):
                        ve.wait_ge(Sm["rowsum_mm"], g // 4 + 1)
                        ve.scalar_tensor_tensor(bs_bc[:, g, :], M[2 + g // 4][:, P * (g % 4):P * (g % 4) + P],
                                                col(vec2, D_LNB + g), bs_bc[:, g, :], ALU.mult, ALU.add
                                                ).then_inc(Sm["bs_ready"], 1)
                if kind == "v" and j == 3:
                    ve.wait_ge(Sm["stats_v"], 8)
                    for r in range(NR):
                        link(ve.bn_aggr(mv[:, r, :], bn[:, r, :, :]))
                    link(ve.tensor_scalar(rinv[:, :], mv[:, :, 1], LN_EPS, None, ALU.add))
                    ve.reciprocal(rinv[:, :], rinv[:, :]).then_inc(Sm["vvar_ready"], 1)
                if kind == "u" and j == 1:
                    ve.wait_ge(Sm["vstd_ready"], 1)
                    for r in range(NR):
                        ve.tensor_scalar(v_rows[:, r, :], v_rows[:, r, :], mv[:, r, 0:1], rstd[:, r:r + 1],
                                         ALU.subtract, ALU.mult).then_inc(Sm["vn_ready"], 1)
                if kind == "za":
                    if j == 0:
                        ve.wait_ge(Sm["bs_ready"], KD)
                    ve.wait_ge(Sm["mixed"], 4)
                    for g in (2 * j, 2 * j + 1):
                        ve.scalar_tensor_tensor(mix[:, g, :].rearrange("p (b i) -> p b i", b=NR),
                                                M[g // 2][:, S * (g % 2):S * (g % 2) + S]
                                                .rearrange("p (b i) -> p b i", b=NR), col(vec2, D_LNG + g),
                                                bs_bc[:, g:g + 1, :].to_broadcast([P, NR, P]), ALU.mult, ALU.add
                                                ).then_inc(Sm["mix_ready"], 1)
                    ve.wait_ge(Sm["mix_ready"], 2 * (j + 1))
                    ve.wait_ge(Sm["u_gated"], j + 1)
                    ve.tensor_tensor(mix[:, 2 * j:2 * j + 2, :], mix[:, 2 * j:2 * j + 2, :],
                                     u_act[:, 2 * j:2 * j + 2, :], ALU.mult).then_inc(Sm["y_a"], 1)
                if kind == "zb":
                    ve.wait_ge(Sm["ya_hi"], j + 1)
                    split_lo(b_lo[:, 2 * j:2 * j + 2, :], mix[:, 2 * j:2 * j + 2, :], b_hi[:, 2 * j:2 * j + 2, :],
                             "ya_lo")
                if c == GN_AT + 5:
                    gn_scale(0)
                if c >= 3:
                    conv_taps(TAPS_A_STEP)
                if c == GN_AT:
                    gn_center(0)
                if c == GN_AT + 3:
                    gn_recip(0)
                if c == GN_AT + 7:
                    y_b(0)
            conv_taps(TAPS * KD)
            c = FIRST["pa"]
            lo(c + 2)
            gn_center(1)

            def drain(c, dst, by):
                ve.wait_ge(Sm["multiplied"], c + 1)
                ve.tensor_tensor(dst, two(U[c % SLOTS][:, :]), by, ALU.mult).then_inc(Sm["dve_drained"], 1)

            def drain_pa(j):
                ve.wait_ge(Sm["act_drained"], drained_count(FIRST["ga"] + j))
                if j == 0:
                    ve.wait_ge(Sm["pT_lo"], 1)
                drain(FIRST["pa"] + j, merged[:, 2 * j:2 * j + 2, :], gate_a[:, 2 * j:2 * j + 2, :])

            drain_pa(0)
            lo(c + 3)
            gn_recip(1)
            gn_scale(1)
            drain_pa(1)
            lo(c + 4)
            y_b(1)
            drain_pa(2)
            for b in range(2):
                ve.wait_ge(Sm["yb_hi"], b + 1)
                four = slice(4 * b, 4 * b + 4)
                split_lo(a_lo[:, four, :], conv[:, four, :], a_hi[:, four, :], "yb_lo")
            lo(c + 5)
            drain_pa(3)
            for j in range(4):
                c = FIRST["pb"] + j
                lo(c + 2)
                ve.wait_ge(Sm["act_drained"], drained_count(FIRST["gb"] + j))
                if j == 3:
                    ve.wait_ge(Sm["mg_added"], 1)
                drain(c, two(tmp[:, j % 3, :]), gate_b[:, 2 * j:2 * j + 2, :])
                ve.wait_ge(Sm["dve_drained"], drained_count(c))
                tiles = merged[:, 2 * j:2 * j + 2, :]
                ve.tensor_tensor(tiles, tiles, two(tmp[:, j % 3, :]), ALU.add).then_inc(Sm["mg_added"], 1)
                ve.wait_ge(Sm["mg_hi"], j + 1)
                split_lo(b_lo[:, 2 * j:2 * j + 2, :], tiles, b_hi[:, 2 * j:2 * j + 2, :], "mg_lo")
            ve.wait_ge(Sm["late_loaded"], 16 * 7)
            ve.tensor_copy(heads_sb.rearrange("b (h a) -> b h a", a=COPIES),
                           relb_sb.rearrange("b (h a) -> b h a", a=1).to_broadcast([32, 2 * HEADS, COPIES])
                           ).then_inc(Sm["heads_ready"], 1)
            lo(FIRST["out"] + 1)
            ve.wait_ge(Sm["bias_rows_T"], 1)
            ve.tensor_copy(rv_sb[:, 0:S], M[4][:, 0:S]).then_inc(Sm["rv_ready"], 1)
            ve.memset(rv_sb[:, S:384], NEG).then_inc(Sm["rv_ready"], 1)
            for j in range(4):
                c = FIRST["out"] + j
                lo(c + 2)
                ve.wait_ge(Sm["multiplied"], c + 1)
                tiles = xT[:, 2 * j:2 * j + 2, :]
                if j == 0:
                    ve.wait_ge(Sm["xT_raw_ready"], 4)
                ve.tensor_tensor(tiles, tiles, two(U[c % SLOTS][:, :]), ALU.add).then_inc(Sm["dve_drained"], 1)
                for k in (2 * j, 2 * j + 1):
                    ve.wait_ge(Sm["x1_hi"], k + 1)
                    ve.scalar_tensor_tensor(a_lo[:, k, :], xT[:, k, :], col(vec, C_PLE + k),
                                            a_hi[:, k, :].bitcast(F32), ALU.mult, ALU.subtract
                                            ).then_inc(Sm["x1_lo"], 1)
            lam = vec2[:, D_LAM:D_LAM + NT]
            ve.scalar_tensor_tensor(sp[:, 0, :], lam, -1.0, lam, ALU.mult, ALU.max).then_inc(Sm["lam_abs"], 1)
            ve.wait_ge(Sm["lam_exp"], 1)
            link(ve.tensor_scalar(sp[:, 2, :], sp[:, 1, :], 2.0, None, ALU.add))
            link(ve.reciprocal(sp[:, 3, :], sp[:, 2, :]))
            link(ve.tensor_tensor(sp[:, 2, :], sp[:, 1, :], sp[:, 3, :], ALU.mult))
            link(ve.tensor_tensor(sp[:, 3, :], sp[:, 2, :], sp[:, 2, :], ALU.mult))
            link(ve.tensor_scalar(sp[:, 4, :], sp[:, 3, :], 1.0 / 15, 1.0 / 13, ALU.mult, ALU.add))
            for odd in (11, 9, 7, 5, 3, 1):
                link(ve.tensor_tensor(sp[:, 4, :], sp[:, 4, :], sp[:, 3, :], ALU.mult))
                link(ve.tensor_scalar(sp[:, 4, :], sp[:, 4, :], 1.0 / odd, None, ALU.add))
            link(ve.scalar_tensor_tensor(sp[:, 4, :], sp[:, 4, :], 2.0, sp[:, 2, :], ALU.mult, ALU.mult))
            link(ve.tensor_scalar(sp[:, 5, :], lam, -1.0, 0.0, ALU.mult, ALU.max))
            link(ve.tensor_tensor(sp[:, 6, :], sp[:, 4, :], sp[:, 5, :], ALU.add))
            ve.tensor_scalar(sp[:, 7, :], sp[:, 6, :], -LRU_C, None, ALU.mult).then_inc(Sm["lam_ready"], 1)
            lo(FIRST["gate"] + 1)
            ve.wait_ge(Sm["r1_std"], 1)
            link(ve.reciprocal(r_bc[:, :], r3_bc[:, :]))
            for j in range(4):
                c = FIRST["gate"] + j
                bc = r_bc[:, :].rearrange("p (a s) -> p a s", a=1).to_broadcast([P, 2, S])
                ve.wait_ge(Sm["multiplied"], c + 1)
                if j == 3:
                    ve.wait_ge(Sm["x2_ready"], 1)
                ve.tensor_tensor(two(tmp[:, j % 3, :]), two(U[c % SLOTS][:, :]), bc, ALU.mult
                                 ).then_inc(Sm["dve_drained"], 1)
                ve.wait_ge(Sm["gate_sig"], j + 1)
                link(ve.tensor_tensor(tmp[:, j % 3, :], tmp[:, j % 3, :], M[j][:, :], ALU.mult))
                tiles = xT[:, 2 * j:2 * j + 2, :]
                ve.tensor_tensor(tiles, tiles, two(tmp[:, j % 3, :]), ALU.add).then_inc(Sm["x2_ready"], 1)
                if j < 3:
                    lo(c + 2)
                for k in (2 * j, 2 * j + 1):
                    ve.wait_ge(Sm["b2_hi"], k + 1)
                    ve.scalar_tensor_tensor(b_lo[:, k, :], xT[:, k, :], col(fm, k),
                                            b_hi[:, k, :].bitcast(F32), ALU.mult, ALU.subtract
                                            ).then_inc(Sm["b2_lo"], 1)
            lo(FIRST["qi"] + 1)
            lo(FIRST["qi"] + 2)
            ve.wait_ge(Sm["s2_std"], 1)
            link(ve.reciprocal(r2_bc[:, :], r3_bc[:, :]))
            link(ve.tensor_tensor(r8_bc[:, :], M[0][:, 0:S], r2_bc[:, :], ALU.mult))
            ve.tensor_tensor(r8_bc[:, :], r8_bc[:, :], r2_bc[:, :], ALU.mult).then_inc(Sm["s3_pre"], 1)
            ve.wait_ge(Sm["s3_std"], 1)
            link(ve.reciprocal(r_bc[:, :], r3_bc[:, :]))
            ve.tensor_tensor(r_bc[:, :], r_bc[:, :], r2_bc[:, :], ALU.mult).then_inc(Sm["rb_ready"], 1)
            ve.wait_ge(Sm["rb_ready"], 1)
            link(ve.tensor_scalar(r8_bc[:, :], r_bc[:, :], DH ** -0.5, None, ALU.mult))
            bc = r_bc[:, :].rearrange("p (a s) -> p a s", a=1).to_broadcast([P, 2, S])
            bc8 = r8_bc[:, :].rearrange("p (a s) -> p a s", a=1).to_broadcast([P, 2, S])

            def score_step(h):
                ve.wait_ge(Sm["relu_done"], h + 1)
                for r, cols in ((1, slice(0, S)), (0, slice(S, S + P))):
                    if h == 0:
                        ve.tensor_scalar(score[:, cols], relu_t[0][:, cols], wi[:, r, 0:1], None, ALU.mult
                                         ).then_inc(Sm["sc_step"], 1)
                    else:
                        ve.wait_ge(Sm["sc_step"], 2 * h - (r == 1))
                        ve.scalar_tensor_tensor(score[:, cols], relu_t[h % 2][:, cols], wi[:, r, h:h + 1],
                                                score[:, cols], ALU.mult, ALU.add).then_inc(Sm["sc_step"], 1)

            topk = [0]

            def top_rounds(n):
                for _ in range(n):
                    i = topk[0]
                    topk[0] += 1
                    views = ((1, score[:, 0:S]), (0, score[:, S:S + P]))
                    for r, v in views:
                        ve.wait_ge(Sm["km_step"], 4 * i - (r == 1)) if i else ve.wait_ge(Sm["sc_step"], 18)
                        ve.max(top8[:, r, :], v).then_inc(Sm["km_step"], 1)
                    for r, v in views:
                        ve.wait_ge(Sm["km_step"], 4 * i + 2 - (r == 1))
                        ve.match_replace(v, top8[:, r, :], v, TAKEN).then_inc(Sm["km_step"], 1)

            def logits(h):
                ve.wait_ge(Sm["s_mm"], h + 1)
                pair = h // 2
                if h < HEADS:
                    ve.wait_ge(Sm["bkm_ready"], 2 * (h + 1))
                    b1, b0 = bkm[h % 2][:, 0:S], bkm[h % 2][:, S:S + P]
                else:
                    wait_bias(ve, pair)
                    bt = bias_t[:, pair % 2, h % 2, :]
                    b1, b0 = bt, bt[:, P:S]
                if h >= 2:
                    ve.wait_ge(Sm["t_mm"], h - 1)
                for r, cols, b in ((1, slice(0, S), b1), (0, slice(S, S + P), b0)):
                    ve.tensor_tensor_reduce(out=z[h % 2][:, cols], in0=M[h % 2][:, cols], in1=b, scale=1.0,
                                            scalar=-3.4e38, op0=ALU.add, op1=ALU.max, accum_out=mx[:, h, r:r + 1]
                                            ).then_inc(Sm["mx_ready"], 1)
                ve.wait_ge(Sm["mx_ready"], 2 * (h + 1))
                ve.tensor_scalar(nmx[:, h, :], mx[:, h, :], -1.0, None, ALU.mult).then_inc(Sm["z_ready"], 1)

            def normalise(h):
                ve.wait_ge(Sm["exp_done"], 2 * (h + 1))
                link(ve.reciprocal(rr[:, h, :], rs[:, h, :]))
                for r, cols in ((1, slice(0, S)), (0, slice(S, S + P))):
                    ve.tensor_scalar(z[h % 2][:, cols], z[h % 2][:, cols], rr[:, h, r:r + 1], None, ALU.mult
                                     ).then_inc(Sm["p_ready"], 1)

            def lo_o(h):
                if h % 2:
                    t = h // 2
                    ve.wait_ge(Sm["o_hi"], t + 1)
                    split_lo(a_lo[:, t, :], M[4][:, S * (t % 2):S * (t % 2) + S], a_hi[:, t, :], "o_lo")

            for c in range(FIRST["qi"] + 1, FIRST["pc2"] + 1):
                kind, j = UNITS[c - 1]
                lo(c + 2)
                d = c - 1
                if kind == "qi":
                    drain(d, qi[:, 2 * j:2 * j + 2, :], bc)
                elif kind == "ki":
                    ve.wait_ge(Sm["rcol_T"], 1)
                    ve.tensor_copy(r_col[:, :], M[3][:, 0:NR]).then_inc(Sm["rcol_ready"], 1)
                    ve.wait_ge(Sm["rcol_ready"], 1)
                    ve.wait_ge(Sm["multiplied"], d + 1)
                    ve.tensor_tensor(ki, U[d % SLOTS][:, 0:S], r_bc[:, :], ALU.mult).then_inc(Sm["rcol_ready"], 1)
                    for r in range(NR):
                        ins = ve.tensor_scalar(wi[:, r, :], U[d % SLOTS][:, S + 8 * r:S + 8 * r + 8],
                                               r_col[:, r:r + 1], None, ALU.mult)
                    ins.then_inc(Sm["dve_drained"], 1)
                elif kind == "xc":
                    if j == 0:
                        ve.memset(xc[:, :, 0:TAPS2 - 1], 0.0).then_inc(Sm["xcc_ready"], 1)
                    drain(d, xc[:, 2 * j:2 * j + 2, TAPS2 - 1:TAPS2 - 1 + S], bc)
                elif kind == "yc":
                    drain(d, two(tmp[:, j, :]), bc)
                elif kind in ("kb", "ka", "qb", "qa"):
                    dst = {"kb": kb, "ka": ka, "qb": qb, "qa": qa}[kind]
                    if kind == "qa" and j == 0:
                        ve.wait_ge(Sm["ri_ready"], NT)
                        ve.wait_ge(Sm["km_ready"], 1)
                    drain(d, dst[:, 2 * j:2 * j + 2, :], bc8 if kind[0] == "q" else bc)
                elif kind in ("vb", "va"):
                    dst = vb if kind == "vb" else va
                    ve.wait_ge(Sm["multiplied"], d + 1)
                    for r in range(NR):
                        ins = ve.tensor_scalar(dst[:, r, S * j:S * j + S], U[d % SLOTS][:, S * r:S * r + S],
                                               r_col[:, r:r + 1], None, ALU.mult)
                    ins.then_inc(Sm["dve_drained"], 1)
                elif kind == "g2":
                    if j >= 3:
                        ve.wait_ge(Sm["g_act"], j - 2)
                    elif j == 0:
                        ve.wait_ge(Sm["yc_act"], 2)
                    drain(d, two(tmp[:, j % 3, :]), bc)
                if kind == "qi" and j == 1:
                    for k in range(KD):
                        ve.scalar_tensor_tensor(xT[:, k, :], xT[:, k, :], col(vec, C_FIN + k), r2_bc[:, :],
                                                ALU.mult, ALU.mult).then_inc(Sm["x3_ready"], 1)
                if IDX_AT < c <= IDX_AT + 4:
                    for h in (2 * (c - IDX_AT - 1), 2 * (c - IDX_AT - 1) + 1):
                        score_step(h)
                if c == IDX_AT + 4:
                    for r, cols in ((1, slice(0, S)), (0, slice(S, S + P))):
                        ve.wait_ge(Sm["sc_step"], 16)
                        ve.wait_ge(Sm["late_loaded"], 16 * 7)
                        ve.scalar_tensor_tensor(score[:, cols], score[:, cols], IDX_SCALE, causal_sb[:, cols],
                                                ALU.mult, ALU.add).then_inc(Sm["sc_step"], 1)
                if kind == "xc" and j == 1:
                    ve.wait_ge(Sm["xcc_ready"], 1)
                    ve.wait_ge(Sm["dve_drained"], drained_count(d))
                    for k in range(TAPS2):
                        for t in range(NT):
                            if k == 0:
                                ve.tensor_scalar(xcc[:, t, :], xc[:, t, 0:S], col(vec2, D_CW2 + t),
                                                 col(vec2, D_CB2 + t), ALU.mult, ALU.add
                                                 ).then_inc(Sm["xcc_ready"], 1)
                            else:
                                ve.wait_ge(Sm["xcc_ready"], NT * (k - 1) + t + 2)
                                ve.scalar_tensor_tensor(xcc[:, t, :], xc[:, t, k:k + S],
                                                        col(vec2, D_CW2 + NT * k + t), xcc[:, t, :], ALU.mult,
                                                        ALU.add).then_inc(Sm["xcc_ready"], 1)
                if TOP_AT <= c < TOP_AT + 4:
                    top_rounds(KEEP // 8 // 4)
                if c == TOP_AT + 4:
                    ve.wait_ge(Sm["km_step"], 4 * (KEEP // 8))
                    ve.tensor_scalar(keep, score, -2e38, NEG, ALU.is_gt, ALU.mult).then_inc(Sm["km_ready"], 2)
                if c == LRU_AT + 2:
                    ve.wait_ge(Sm["lru_act"], NT)
                    ve.wait_ge(Sm["ri_act"], NT)
                    link(ve.tensor_tensor(lru_r, lru_a, lru_a, ALU.mult))
                    ve.scalar_tensor_tensor(lru_b, lru_r, 1.0, lru_b, ALU.add, ALU.mult
                                            ).then_inc(Sm["lru_dve"], 1)
                    ve.tensor_tensor(lru_i, lru_i, xcc, ALU.mult).then_inc(Sm["lru_dve"], 1)
                if c == LRU_AT + 4:
                    ve.wait_ge(Sm["lru_act"], NT + 1)
                    link(ve.tensor_tensor(lru_i, lru_i, lru_b, ALU.mult))
                    for t in range(NT):
                        ins = ve.tensor_tensor_scan(lru_r[:, t, :], lru_a[:, t, :], lru_i[:, t, :], 0.0,
                                                    ALU.mult, ALU.add)
                    ins.then_inc(Sm["lru_dve"], 1)
                    ve.wait_ge(Sm["lru_dve"], 3)
                    ve.wait_ge(Sm["yc_act"], 2)
                    ve.tensor_tensor(lru_a, lru_r, yc, ALU.mult).then_inc(Sm["lru_dve"], 1)
                if c == LRU_AT + 5:
                    ve.wait_ge(Sm["yc_hi"], 1)
                    split_lo(c_lo[:, :, :], lru_a, c_hi[:, :, :], "yc_lo")
                h = c - HEAD_AT
                if 0 <= h < 16:
                    logits(h)
                if 0 <= h < 16:
                    normalise(h)
                if 2 <= h < 18:
                    lo_o(h - 2)

            ve.wait_ge(Sm["g_act"], 12)
            for n in range(6):
                kind, j = UNITS[FIRST["pc2"] + n]
                c = FIRST["pc2"] + n
                g0 = KD * {"pc2": 2, "pb2": 1, "pa2": 0}[kind]
                ve.wait_ge(Sm["multiplied"], c + 1)
                for half in range(2):
                    t = 4 * j + 2 * half
                    src = U[c % SLOTS] if half == 0 else M[c % SLOTS]
                    tiles = merged[:, t:t + 2, :]
                    by = gates2[:, g0 + t:g0 + t + 2, :]
                    dst = tiles if kind == "pc2" else two(tmp[:, half, :])
                    ins = ve.scalar_tensor_tensor(dst, by, 1.0, two(src[:, :]), ALU.add, ALU.mult)
                    if half == 0:
                        chain[0] += 1
                        ins.then_inc(Sm["vchain"], 1)
                    else:
                        ins.then_inc(Sm["dve_drained"], 1)
                if kind != "pc2":
                    for half in range(2):
                        t = 4 * j + 2 * half
                        tiles = merged[:, t:t + 2, :]
                        if half == 0:
                            ve.wait_ge(Sm["vchain"], chain[0])
                        else:
                            ve.wait_ge(Sm["dve_drained"], drained_count(c))
                        ins = ve.tensor_tensor(tiles, tiles, two(tmp[:, half, :]), ALU.add)
                        if kind == "pb2":
                            link(ins)
                        else:
                            ins.then_inc(Sm["mg_added"], 1)
                    if kind == "pa2":
                        for half in range(2):
                            t = 4 * j + 2 * half
                            ve.wait_ge(Sm["m2_hi"], 2 * j + half + 1)
                            ve.scalar_tensor_tensor(b_lo[:, t:t + 2, :], merged[:, t:t + 2, :], 0.5,
                                                    b_hi[:, t:t + 2, :].bitcast(F32), ALU.mult, ALU.subtract
                                                    ).then_inc(Sm["m2_lo"], 1)
                else:
                    ve.wait_ge(Sm["vchain"], chain[0])
                    ve.wait_ge(Sm["dve_drained"], drained_count(c))
                lo(c + 3)
            for j in range(4):
                c = FIRST["wo"] + j
                ve.wait_ge(Sm["multiplied"], c + 1)
                tiles = xT[:, 2 * j:2 * j + 2, :]
                if j == 0:
                    ve.wait_ge(Sm["x3_ready"], KD)
                ve.tensor_tensor(tiles, tiles, two(U[c % SLOTS][:, :]), ALU.add).then_inc(Sm["dve_drained"], 1)
                for k in (2 * j, 2 * j + 1):
                    ve.wait_ge(Sm["x4_hi"], k + 1)
                    ve.scalar_tensor_tensor(a_lo[:, k, :], xT[:, k, :], col(vec2, D_MLP + k),
                                            a_hi[:, k, :].bitcast(F32), ALU.mult, ALU.subtract
                                            ).then_inc(Sm["x4_lo"], 1)
                if j < 2:
                    lo(c + 3)
            lo(UP0 + 1)
            lo(UP0 + 2)
            ve.wait_ge(Sm["r4_ssq"], NR)
            link(ve.tensor_scalar(rinv[:, :], ssq[:, :], 1.0 / D, EPS, ALU.mult, ALU.add))
            ve.reciprocal(rr[:, 0, :], rinv[:, :]).then_inc(Sm["r4_ready"], 1)

            def squares(drained, count, slot):
                ve.wait_ge(Sm["act_drained"], drained)
                ve.tensor_tensor(tmp[:, 1, :], tmp[:, 0, :], tmp[:, 0, :], ALU.mult).then_inc(Sm["sq_up"], 1)
                ve.wait_ge(Sm["h_hi"], count)
                split_lo(b_lo[:, 2 * slot:2 * slot + 2, :], two(tmp[:, 1, :]), b_hi[:, 2 * slot:2 * slot + 2, :],
                         "h_lo")

            act0 = drained_count(UP0)
            squares(act0, 1, 0)

            def loop_body(i, last=False):
                for q in range(PAIRS_A_TURN):
                    for half in range(2):
                        c = LOOP0 + 2 * q + half
                        if half == 1:
                            squares(3 * i + (act0 + q + 1), 3 * i + (q + 2), (q + 1) % 3)
                        n = c + 2
                        if not (last and n > LOOP0 + 6):
                            ve.wait_ge(Sm["hi_ready"], 6 * i + (n + 1))
                            ve.tensor_tensor(wlo[:, n % SLOTS, :], raw[:, n % SLOTS, :],
                                             whi[:, n % SLOTS, :].bitcast(F32), ALU.subtract
                                             ).then_inc(Sm["lo_ready"], 1)

            with ve.Fori(0, LOOP_PAIRS // PAIRS_A_TURN - 1) as i:
                loop_body(i)
            loop_body(LOOP_PAIRS // PAIRS_A_TURN - 1, last=True)
            ve.wait_ge(Sm["r4_ready"], 1)
            ve.wait_ge(Sm["x4_copied"], 4)
            for r in range(NR):
                ve.wait_ge(Sm["y_mm"], r + 1)
                for half in range(2):
                    cols = slice(512 * half, 512 * half + 512)
                    ins = ve.scalar_tensor_tensor(y_rows[:, r, cols], M[2 * r + half][:, :], rr[:, 0, r:r + 1],
                                                  x4_rows[:, r, cols], ALU.mult, ALU.add)
                    if half == 0:
                        chain[0] += 1
                        ins.then_inc(Sm["vchain"], 1)
                ins.then_inc(Sm["fin_y"], 1)
            ve.wait_ge(Sm["late_loaded"], 16 * 8)
            for r in range(NR):
                ve.wait_ge(Sm["fin_ssq"], r + 1)
                link(ve.tensor_scalar(rinv[:, r:r + 1], ssq[:, r:r + 1], 1.0 / D, EPS, ALU.mult, ALU.add))
                ve.reciprocal(rinv[:, r:r + 1], rinv[:, r:r + 1]).then_inc(Sm["fin_inv"], 1)
                ve.wait_ge(Sm["fin_std"], r + 1)
                for half in range(2):
                    cols = slice(512 * half, 512 * half + 512)
                    ve.scalar_tensor_tensor(y_rows[:, r, cols], y_rows[:, r, cols], rstd[:, r:r + 1],
                                            fin_bc[:, cols], ALU.mult, ALU.mult).then_inc(Sm["fin_out"], 1)

        @block.tensor
        def _(pe):
            def rows_T(src, k, r, dst):
                return pe.transpose(dst, src[:, r, P * k:P * k + P], ident[:, :])

            def begin(c):
                pe.wait_ge(Sm["lo_ready"], c + 1)
                if shared(c):
                    pe.wait_ge(Sm["pool_lo_ready"], pool_count(c))
                b = c - SLOTS
                while b >= 0 and UNITS[b][0] in ("ple", "ple2"):
                    b -= SLOTS
                if b >= 0:
                    which = "act_drained" if UNITS[b][0] in ACT_DRAINS else "dve_drained"
                    pe.wait_ge(Sm[which], drained_count(b))

            def product(dst, stationary, moving, kt, first=True):
                for k in range(kt):
                    (sh, sl), (mh, ml) = stationary(k), moving(k)
                    pe.matmul(dst, sh, mh, start=first and k == 0, stop=False)
                    pe.matmul(dst, sh, ml, start=False, stop=False)
                    ins = pe.matmul(dst, sl, mh, start=False, stop=k == kt - 1)
                return ins

            def weights(slot, kt, n0, n1):
                h, l = slot3w(whi, slot, kt), slot3w(wlo, slot, kt)
                return lambda k: (h[:, k, n0:n1], l[:, k, n0:n1])

            def slot3w(ring, slot, kt):
                words = UW if kt != 2 else 1024
                return ring[:, slot, 0:words].rearrange("p (k n) -> p k n", k=kt)

            def tiles(h, l, t0=0):
                return lambda k: (h[:, t0 + k, :], l[:, t0 + k, :])

            def row_tiles(h, l, r, t0=0):
                return lambda k: (h[:, t0 + k, P * r:P * r + P], l[:, t0 + k, P * r:P * r + P])

            def columns(c, h, l, kt=KD, t0=0):
                begin(c)
                for n in range(2):
                    ins = product(U[c % SLOTS][:, S * n:S * n + S], weights(c % SLOTS, kt, P * n, P * n + P),
                                  tiles(h, l, t0), kt)
                ins.then_inc(Sm["multiplied"], 1)

            def arriving(units, h, l, arrive, early=6, between=None):
                def tile_products(c, k):
                    hs, ls = slot3w(whi, c % SLOTS, KD), slot3w(wlo, c % SLOTS, KD)
                    for n in range(2):
                        dst, cols = U[c % SLOTS][:, S * n:S * n + S], slice(P * n, P * n + P)
                        pe.matmul(dst, hs[:, k, cols], h[:, k, :], start=k == 0 and n == 0, stop=False,
                                  skip_group_check=True)
                        pe.matmul(dst, ls[:, k, cols], h[:, k, :], start=False, stop=False, skip_group_check=True)
                        arrive(k, 1)
                        ins = pe.matmul(dst, hs[:, k, cols], l[:, k, :], start=False, stop=k == KD - 1,
                                        skip_group_check=True)
                    return ins
                for c in units:
                    begin(c)
                    for k in range(early):
                        arrive(k, 0)
                        tile_products(c, k)
                if between is not None:
                    between()
                for c in units:
                    for k in range(early, KD):
                        arrive(k, 0)
                        ins = tile_products(c, k)
                    ins.then_inc(Sm["multiplied"], 1)

            def arrival(hi_done, lo_done, tiles_each=1, before=0):
                def arrive(k, part):
                    pe.wait_ge(Sm[lo_done if part else hi_done], before + k // tiles_each + 1)
                return arrive

            def rows_out(c, h, l, bias=None):
                begin(c)
                for r in range(NR):
                    dst = U[c % SLOTS][:, S * r:S * r + S]
                    if bias is not None:
                        pe.matmul(dst, ones[0:1, :], bias, start=True, stop=False)
                    ins = product(dst, row_tiles(h, l, r), weights(c % SLOTS, KD, 0, S), KD, first=bias is None)
                ins.then_inc(Sm["multiplied"], 1)

            pe.wait_ge(Sm["consts"], 9)
            def vectors_T(tile, n, at):
                pe.transpose(M[4][:, at:at + n], vec_rows[0:n, tile, :], ident[0:n, 0:n]).then_inc(Sm["vecs_T"], 1)

            for r in range(NR):
                pe.wait_ge(Sm[f"x_loaded{r}"], 16)
                for k in range(KD):
                    ins = rows_T(x_rows, k, r, M[k // 2][:, S * (k % 2) + P * r:S * (k % 2) + P * r + P])
                    if r == NR - 1 and k % 2:
                        ins.then_inc(Sm["xT_raw"], 1)
            for r in range(NR):
                pe.wait_ge(Sm["diag_ready"], r + 1)
                ins = pe.matmul(U[2][:, P * r:P * r + P], ones[:, :], diag[:, r, :], start=True, stop=True)
            ins.then_inc(Sm["rbc_ready"], 1)
            pe.wait_ge(Sm["vec_loaded"], 16 * 8)
            vectors_T(0, 120, 0)
            pe.wait_ge(Sm["vec2_loaded"], 16 * 10)
            pe.wait_ge(Sm["vecs_ready"], 1)
            for tile, n, at in ((1, P, 128), (2, 120, 256), (3, 56, 384)):
                vectors_T(tile, n, at)

            def conv_mean(b):
                pe.wait_ge(Sm["tap"], TAPS * NT * (b + 1))
                if b == 0:
                    pe.wait_ge(Sm["mix_ready"], KD)
                else:
                    pe.wait_ge(Sm["hn_ready"], 2)
                for t in range(NT):
                    ins = pe.matmul(M[t // 2][:, S * (t % 2):S * (t % 2) + S], o128[:, :], conv[:, 4 * b + t, :],
                                    start=True, stop=True)
                    if t % 2:
                        ins.then_inc(Sm["conv_mean"], 1)

            def conv_var(b):
                pe.wait_ge(Sm["gsq_ready"], b + 1)
                for t in range(NT):
                    ins = pe.matmul(M[2][0:NT, 0:S], sel_var[:, t, :], gn_sq[:, t, :], start=t == 0, stop=t == NT - 1)
                ins.then_inc(Sm["gvar_ready"], 1)

            def conv_bc(b):
                pe.wait_ge(Sm["grcp_ready"], b + 1)
                pe.wait_ge(Sm["d_ready"], 2 * (b + 1))
                for t in range(NT):
                    ins = pe.matmul(M[t // 2][:, S * (t % 2):S * (t % 2) + S], sel_bc[:, t, :], gr,
                                    start=True, stop=True)
                    if t % 2:
                        ins.then_inc(Sm["gbc_ready"], 1)

            for c in range(FIRST["pa"]):
                kind, j = UNITS[c]
                if kind == "v":
                    if j == 0:
                        pe.wait_ge(Sm["early_loaded"], 64)
                    rows_out(c, a_hi, a_lo, bias_v[:, S * j:S * j + S])
                elif c == 0:
                    arriving([c], a_hi, a_lo, arrival("in_hi", "in_lo"))
                else:
                    columns(c, a_hi, a_lo)
                if c == 0:
                    pe.wait_ge(Sm["vecs_ready"], 4)
                    pe.wait_ge(Sm["early_loaded"], 64)
                    for k in range(2):
                        for r in range(NR):
                            ins = rows_T(p_rows, k, r, M[4][:, S * k + P * r:S * k + P * r + P])
                    ins.then_inc(Sm["pT_ready"], 1)
                if c == 5:
                    pe.wait_ge(Sm["xT_raw_ready"], 4)
                    for g in range(KD):
                        ins = pe.transpose(M[g // 4][:, P * (g % 4):P * (g % 4) + P], ws_rows[:, g, :], ident[:, :])
                        if g % 4 == 3:
                            ins.then_inc(Sm["wsT_ready"], 1)
                if c == 8:
                    pe.wait_ge(Sm["wsT_sb"], 3)
                    for h in range(2):
                        pe.matmul(M[2 + h][:, :], ones[:, :], wsT[:, 4 * h:4 * h + 4, :], start=True, stop=True
                                  ).then_inc(Sm["rowsum_mm"], 1)
                if c == 15:
                    pe.wait_ge(Sm["vn_ready"], NR)
                    pe.wait_ge(Sm["bs_ready"], KD)
                    for g in range(KD):
                        for r in range(NR):
                            ins = pe.matmul(M[g // 2][:, S * (g % 2) + P * r:S * (g % 2) + P * r + P],
                                            v_rows[:, r, P * g:P * g + P], wsT[:, g, :], start=True, stop=True)
                        if g % 2:
                            ins.then_inc(Sm["mixed"], 1)
                if c == GN_AT - 1:
                    conv_mean(0)
                if c == GN_AT + 1:
                    conv_var(0)
                if c == GN_AT + 4:
                    conv_bc(0)
            conv_mean(1)
            pe.wait_ge(Sm["ya_lo"], 4)
            columns(FIRST["pa"], b_hi, b_lo)
            pe.wait_ge(Sm["gstd_ready"], 1)
            conv_var(1)
            columns(FIRST["pa"] + 1, b_hi, b_lo)
            conv_bc(1)
            columns(FIRST["pa"] + 2, b_hi, b_lo)
            columns(FIRST["pa"] + 3, b_hi, b_lo)
            pe.wait_ge(Sm["yb_lo"], 2)
            for j in range(4):
                columns(FIRST["pb"] + j, a_hi, a_lo)

            def per_layer(c, bank):
                pe.wait_ge(Sm["lo_ready"], c + 1)
                for n in range(4):
                    ins = product(M[bank + n // 2][:, S * (n % 2):S * (n % 2) + S],
                                  weights(c % SLOTS, 2, P * n, P * n + P), tiles(c_hi, c_lo), 2)
                ins.then_inc(Sm["multiplied"], 1)

            pe.wait_ge(Sm["pT_lo"], 1)
            pe.wait_ge(Sm["hn_ready"], 4)
            per_layer(FIRST["ple"], 0)
            pe.wait_ge(Sm["late_loaded"], 16 * 7)
            pe.wait_ge(Sm["heads_ready"], 1)
            pe.matmul(M[4][:, 0:S], heads_sb, onehot_sb[:, 0:S], start=True, stop=True
                      ).then_inc(Sm["bias_rows_T"], 1)
            arriving([FIRST["out"]], b_hi, b_lo, arrival("mg_hi", "mg_lo", 2))
            for j in range(1, 4):
                columns(FIRST["out"] + j, b_hi, b_lo)
            pe.wait_ge(Sm["gstd_ready"], 2)
            per_layer(FIRST["ple2"], 2)

            def mean_square():
                pe.wait_ge(Sm["sq_summed"], 3)
                pe.wait_ge(Sm["rv_ready"], 2)
                for k in range(2):
                    ins = pe.matmul(M[4][:, 0:S], o1024[:, :], sq1[:, k, :], start=k == 0, stop=k == 1)
                ins.then_inc(Sm["ms_ready"], 1)

            arriving([FIRST["gate"]], a_hi, a_lo, arrival("x1_hi", "x1_lo"), between=mean_square)
            for j in range(1, 4):
                columns(FIRST["gate"] + j, a_hi, a_lo)
            pe.wait_ge(Sm["r1_std"], 1)
            for j in range(4):
                pe.wait_ge(Sm["x2_ready"], 1)
                pe.wait_ge(Sm["sq12"], j + 1)
                for dst, sq in ((M[4], sq1), (M[0], sq2)):
                    for k in (2 * j, 2 * j + 1):
                        ins = pe.matmul(dst[:, 0:S], o1024[:, :], sq[:, k, :], start=k == 0, stop=k == KD - 1)
            ins.then_inc(Sm["ms2_ready"], 1)
            pe.wait_ge(Sm["b2_lo"], KD)

            def dots(h):
                if h >= 4:
                    pe.wait_ge(Sm["relu_done"], h - 3)
                q = slice(DH * (h % 2), DH * (h % 2) + DH)
                pe.matmul(M[h % 4][:, 0:S], qi[q, h // 2, P:S], ki[q, :], start=True, stop=True)
                pe.matmul(M[h % 4][:, S:S + P], qi[q, h // 2, 0:P], ki[q, 0:P], start=True, stop=True
                          ).then_inc(Sm["dots"], 1)

            def scores(h):
                q_, k_ = (qb, kb) if h < HEADS else (qa, ka)
                t, q = (h % HEADS) // 2, slice(DH * (h % 2), DH * (h % 2) + DH)
                if h in (0, HEADS):
                    pe.wait_ge(Sm["dve_drained"], drained_count(FIRST["vb" if h == 0 else "va"] + 1))
                if h >= 2:
                    pe.wait_ge(Sm["z_ready"], h - 1)
                else:
                    pe.wait_ge(Sm["ri_act"], NT)
                pe.matmul(M[h % 2][:, 0:S], q_[q, t, P:S], k_[q, t, :], start=True, stop=True)
                pe.matmul(M[h % 2][:, S:S + P], q_[q, t, 0:P], k_[q, t, 0:P], start=True, stop=True
                          ).then_inc(Sm["s_mm"], 1)

            def probs_T(h):
                pe.wait_ge(Sm["p_ready"], 2 * (h + 1))
                if h >= 2:
                    pe.wait_ge(Sm["pT_copied"], h - 1)
                for n, at in enumerate((S, 0, P)):
                    ins = pe.transpose(M[2 + h % 2][:, P * n:P * n + P], z[h % 2][:, at:at + P], ident[:, :])
                ins.then_inc(Sm["t_mm"], 1)

            def values(h):
                v = vb if h < HEADS else va
                t, q = h // 2, slice(DH * (h % 2), DH * (h % 2) + DH)
                cols = slice(DH * (h % HEADS), DH * (h % HEADS) + DH)
                pe.wait_ge(Sm["pT_copied"], h + 1)
                if t >= 1:
                    pe.wait_ge(Sm["o_lo"], t)
                a = S * (t % 2)
                pe.matmul(M[4][q, a:a + S], v[:, 0, cols], pT[h % 2][:, 0:S], start=True, stop=False)
                pe.matmul(M[4][q, a + P:a + S], v[:, 1, cols], pT[h % 2][:, S:S + P], start=False, stop=True
                          ).then_inc(Sm["pv_mm"], 1)

            def attention(c):
                h = c - HEAD_AT
                if 0 <= h < 16:
                    scores(h)
                if 1 <= h < 17:
                    probs_T(h - 1)
                if 2 <= h < 18:
                    values(h - 2)

            for c in range(FIRST["qi"], FIRST["pc2"]):
                kind, j = UNITS[c]
                if kind in ("vb", "va"):
                    rows_out(c, b_hi, b_lo)
                elif kind == "ki":
                    begin(c)
                    product(U[c % SLOTS][:, 0:S], weights(c % SLOTS, KD, 0, P), tiles(b_hi, b_lo), KD)
                    for r in range(NR):
                        ins = product(U[c % SLOTS][:, S + HEADS * r:S + HEADS * r + HEADS], row_tiles(b_hi, b_lo, r),
                                      weights(c % SLOTS, KD, P, P + HEADS), KD)
                    ins.then_inc(Sm["multiplied"], 1)
                else:
                    columns(c, b_hi, b_lo)
                if c == FIRST["qi"] + 1:
                    pe.wait_ge(Sm["rb_ready"], 1)
                    pe.wait_ge(Sm["x2_ready"], 4)
                    for r in range(NR):
                        ins = pe.matmul(M[3][:, r:r + 1], r_bc[0:1, P * r:P * r + P], ones[0:1, 0:1], start=True,
                                        stop=True)
                    ins.then_inc(Sm["rcol_T"], 1)
                if IDX_AT <= c < IDX_AT + 4:
                    if c == IDX_AT:
                        pe.wait_ge(Sm["dve_drained"], drained_count(FIRST["ki"]))
                    dots(2 * (c - IDX_AT))
                    dots(2 * (c - IDX_AT) + 1)
                if c == LRU_AT:
                    pe.wait_ge(Sm["relu_done"], HEADS)
                    pe.wait_ge(Sm["xcc_ready"], 1 + NT * TAPS2)
                    pe.wait_ge(Sm["late_loaded"], 16 * 7)
                    for t in range(NT):
                        for w in range(2):
                            ins = pe.matmul(M[t][:, S * w:S * w + S], w_gates[:, w, t, :], xcc[:, t, :], start=True,
                                            stop=True)
                        ins.then_inc(Sm["ri_ready"], 1)
                attention(c)

            def branch(c, h, l, t0):
                begin(c)
                if c >= FIRST["pc2"] + SLOTS:
                    pe.wait_ge(Sm["dve_drained"], drained_count(c - SLOTS))
                for n in range(4):
                    bank = (U if n < 2 else M)[c % SLOTS]
                    ins = product(bank[:, S * (n % 2):S * (n % 2) + S], weights(c % SLOTS, 4, P * n, P * n + P),
                                  tiles(h, l, t0), 4)
                ins.then_inc(Sm["multiplied"], 1)

            pe.wait_ge(Sm["yc_lo"], 1)
            branch(FIRST["pc2"], c_hi, c_lo, 0)
            attention(FIRST["pc2"])
            branch(FIRST["pc2"] + 1, c_hi, c_lo, 0)
            pe.wait_ge(Sm["o_lo"], 4)
            branch(FIRST["pb2"], a_hi, a_lo, 0)
            branch(FIRST["pb2"] + 1, a_hi, a_lo, 0)
            pe.wait_ge(Sm["o_lo"], 8)
            branch(FIRST["pa2"], a_hi, a_lo, 4)
            branch(FIRST["pa2"] + 1, a_hi, a_lo, 4)
            arriving([FIRST["wo"], FIRST["wo"] + 1], b_hi, b_lo, arrival("m2_hi", "m2_lo", 2), early=4)
            for j in range(2, 4):
                columns(FIRST["wo"] + j, b_hi, b_lo)

            def residual_T():
                pe.wait_ge(Sm["dve_drained"], drained_count(FIRST["wo"] + 3))
                for k in range(KD):
                    for r in range(NR):
                        at = S * (k % 2) + P * r
                        ins = pe.transpose(M[k // 2][:, at:at + P], xT[:, k, P * r:P * r + P], ident[:, :])
                    if k % 2:
                        ins.then_inc(Sm["x4T"], 1)

            def up_block(slot):
                for n in range(2):
                    ins = product(U[slot][:, S * n:S * n + S], weights(slot, KD, P * n, P * n + P),
                                  tiles(a_hi, a_lo), KD)
                ins.then_inc(Sm["multiplied"], 1)

            def down_block(slot, h0, first, last):
                wh = whi[:, slot, :].rearrange("p (k n) -> p k n", k=2)
                wl = wlo[:, slot, :].rearrange("p (k n) -> p k n", k=2)
                for r in range(NR):
                    rows = slice(P * r, P * r + P)
                    for half in range(2):
                        cols = slice(512 * half, 512 * half + 512)
                        dst = M[2 * r + half][:, :]
                        for k in range(2):
                            hh, hl = b_hi[:, h0 + k, rows], b_lo[:, h0 + k, rows]
                            pe.matmul(dst, hh, wh[:, k, cols], start=first and k == 0, stop=False,
                                      skip_group_check=True)
                            pe.matmul(dst, hl, wh[:, k, cols], start=False, stop=False, skip_group_check=True)
                            ins = pe.matmul(dst, hh, wl[:, k, cols], start=False, stop=last and k == 1,
                                            skip_group_check=True)
                    if last:
                        ins.then_inc(Sm["y_mm"], 1)
                if not last:
                    ins.then_inc(Sm["multiplied"], 1)

            act0 = drained_count(UP0)
            arriving([UP0], a_hi, a_lo, arrival("x4_hi", "x4_lo"), between=residual_T)

            def pairs(i, first=False):
                for q in range(PAIRS_A_TURN):
                    c = LOOP0 + 2 * q
                    pe.wait_ge(Sm["lo_ready"], 6 * i + (c + 1))
                    pe.wait_ge(Sm["act_drained"], 3 * i + (act0 + q - 1))
                    up_block(c % SLOTS)
                    if first and q == 0:
                        pe.wait_ge(Sm["x4_copied"], 4)
                    pe.wait_ge(Sm["lo_ready"], 6 * i + (c + 2))
                    pe.wait_ge(Sm["h_lo"], 3 * i + (q + 1))
                    down_block((c + 1) % SLOTS, 2 * q, first and q == 0, False)

            pairs(0, first=True)
            with pe.Fori(1, LOOP_PAIRS // PAIRS_A_TURN) as i:
                pairs(i)
            c = len(UNITS) - 1
            pe.wait_ge(Sm["lo_ready"], c + 1)
            pe.wait_ge(Sm["h_lo"], LOOP_PAIRS + 1)
            down_block(c % SLOTS, 2 * (LOOP_PAIRS % 3), False, True)


_INS = ["x", "p", "norm_g", "w_in", "b_in", "a_ln_g", "a_ln_b", "a_ws", "a_bs", "b_conv_w", "b_conv_b", "b_gn_g",
        "b_gn_b", "w_pa", "w_pb", "w_out", "ple_norm_g", "w_ple_gate", "w_ple", "final_g", "rel_bias_2",
        "norm_mix_g_2", "w_in_2", "conv_w_2", "conv_b_2", "w_r_2", "b_r_2", "w_i_2", "b_i_2", "lru_lambda_2",
        "w_pa_2", "w_pb_2", "w_pc_2", "w_o_2", "norm_mlp_g_2", "w_up_2", "w_down_2", "final_norm_g_2"]


def distance_buckets():
    n = 255 - np.arange(384)
    nf = np.maximum(n, 1).astype(np.float32)
    large = 16 + (np.log(nf / np.float32(16)) / np.float32(np.log(8.0)) * np.float32(16)).astype(np.int32)
    bucket = np.where(n < 16, np.maximum(n, 0), np.minimum(large, 31))
    return ((np.arange(32)[:, None] == bucket[None, :]) & (n >= 0)[None, :]).astype(np.float32)


def causal_tile():
    row, key = np.arange(P)[:, None], np.arange(S)[None, :]
    one = np.where(key <= P + row, 0.0, NEG)
    zero = np.where(key[:, :P] <= row, 0.0, NEG)
    return np.concatenate([one, zero], axis=1).astype(np.float32)


def kernel(**inputs):
    import concourse.bacc as bacc
    from concourse.bass_utils import run_bass_kernel_spmd

    nc = bacc.Bacc("TRN2", target_bir_lowering=False, num_devices=1)
    arrays = {f"in_{n}": np.ascontiguousarray(inputs[n]) for n in _INS}
    arrays["onehot"] = distance_buckets()
    arrays["causal"] = causal_tile()
    aps = {n: nc.dram_tensor(n, a.shape, mybir.dt.from_np(a.dtype), kind="ExternalInput").ap()
           for n, a in arrays.items()}
    scratch = nc.dram_tensor("bias_by_distance", [P, P // COPIES, BW], F32).ap()
    out = nc.dram_tensor("out", [1, S, D], F32, kind="ExternalOutput").ap()
    block_program(nc, {n: aps[f"in_{n}"] for n in _INS}, aps["onehot"], aps["causal"], scratch, out)
    r = run_bass_kernel_spmd(nc, [arrays], core_ids=[0])
    return r.results[0]["out"]
```
